# Optimizing a Trainium2 kernel written in Bass

```python
import jax
import jax.numpy as jnp
from jax import lax
import numpy as np
import math
import jax, jax.numpy as jnp

D_MODEL = 2048
BATCH = 1
SEQ = 256
DEPTH = 2

MIX_WIDTH = 2048
CONV_WIDTH = 1024
CONV_KERNEL = 31
MOBA_HEADS = 8
MOBA_HEAD_DIM = 128
MOBA_WIDTH = MOBA_HEADS * MOBA_HEAD_DIM
MOBA_BLOCK = 256
MOBA_TOPK = 3
MOBA_QCHUNK = 32
EVEN_IN = 3 * CONV_WIDTH + 4 * MOBA_WIDTH
DSA_HEADS = 16
DSA_HEAD_DIM = 128
DSA_WIDTH = DSA_HEADS * DSA_HEAD_DIM
Q_LORA = 512
KV_LORA = 256
IDX_HEADS = 16
IDX_DIM = 64
DSA_TOPK_MAX = 256
DSA_QCHUNK = 128
ODD_IN = Q_LORA + KV_LORA + IDX_DIM + IDX_HEADS + DSA_WIDTH
N_EVEN = (DEPTH + 1) // 2
N_ODD = DEPTH // 2
EPS = 1e-6


def _rmsnorm(x, g):
    xf = x.astype(jnp.float32)
    y = xf * lax.rsqrt(jnp.mean(xf * xf, axis=-1, keepdims=True) + EPS)
    return (y * g.astype(jnp.float32)).astype(x.dtype)

def _layernorm(x, g, b):
    xf = x.astype(jnp.float32)
    mu = jnp.mean(xf, axis=-1, keepdims=True)
    xc = xf - mu
    y = xc * lax.rsqrt(jnp.mean(xc * xc, axis=-1, keepdims=True) + EPS)
    return (y * g.astype(jnp.float32) + b.astype(jnp.float32)).astype(x.dtype)

def _split_cols(z, sizes):
    out = []
    off = 0
    for s in sizes:
        out.append(z[..., off:off + s])
        off += s
    return out

def _conformer_conv(a_val, a_gt, w_dw, b_dw, ln_g, ln_b, w_pw, b_pw):
    u = a_val * jax.nn.sigmoid(a_gt)
    y = lax.conv_general_dilated(
        u, w_dw[:, None, :], window_strides=(1,), padding=[(CONV_KERNEL - 1, 0)],
        dimension_numbers=('NWC', 'WIO', 'NWC'), feature_group_count=CONV_WIDTH) + b_dw
    y = jax.nn.silu(_layernorm(y, ln_g, ln_b))
    return y @ w_pw + b_pw

def _moba_attention(q, k, v):
    b, t, h, dh = q.shape
    nb = -(-t // MOBA_BLOCK)
    pad = nb * MOBA_BLOCK - t
    q = q.transpose(0, 2, 1, 3)
    k = jnp.pad(k.transpose(0, 2, 1, 3), ((0, 0), (0, 0), (0, pad), (0, 0)))
    v = jnp.pad(v.transpose(0, 2, 1, 3), ((0, 0), (0, 0), (0, pad), (0, 0)))
    kb = k.reshape(b, h, nb, MOBA_BLOCK, dh)
    vb = v.reshape(b, h, nb, MOBA_BLOCK, dh)
    n_sel = min(MOBA_TOPK, nb - 1)
    scale = dh ** -0.5
    sel = None
    if n_sel > 0:
        k_mean = jnp.mean(kb, axis=3)
        gate = jnp.einsum('bhtd,bhnd->bhtn', q, k_mean)
        cur = jnp.arange(t) // MOBA_BLOCK
        fully_past = jnp.arange(nb)[None, :] < cur[:, None]
        gate = jnp.where(fully_past, gate, -jnp.inf)
        sel = lax.top_k(gate, n_sel)[1]
    bi = jnp.arange(b)[:, None, None, None]
    hi = jnp.arange(h)[None, :, None, None]

    def chunk(c):
        t0 = c * MOBA_QCHUNK
        blk = t0 // MOBA_BLOCK
        qc = lax.dynamic_slice_in_dim(q, t0, MOBA_QCHUNK, axis=2)
        k_own = lax.dynamic_index_in_dim(kb, blk, axis=2, keepdims=False)
        v_own = lax.dynamic_index_in_dim(vb, blk, axis=2, keepdims=False)
        qpos = t0 + jnp.arange(MOBA_QCHUNK)
        kpos = blk * MOBA_BLOCK + jnp.arange(MOBA_BLOCK)
        s_own = jnp.einsum('bhqd,bhsd->bhqs', qc, k_own) * scale
        s_own = jnp.where(kpos[None, :] <= qpos[:, None], s_own, -jnp.inf)
        if n_sel == 0:
            p = jax.nn.softmax(s_own.astype(jnp.float32), axis=-1).astype(v.dtype)
            return jnp.einsum('bhqs,bhsd->bhqd', p, v_own)
        sel_c = lax.dynamic_slice_in_dim(sel, t0, MOBA_QCHUNK, axis=2)
        k_sel = kb[bi, hi, sel_c]
        v_sel = vb[bi, hi, sel_c]
        s_past = jnp.einsum('bhqd,bhqksd->bhqks', qc, k_sel) * scale
        s_past = jnp.where((sel_c < blk)[..., None], s_past, -jnp.inf)
        logits = jnp.concatenate(
            [s_past.reshape(b, h, MOBA_QCHUNK, n_sel * MOBA_BLOCK), s_own], axis=-1)
        p = jax.nn.softmax(logits.astype(jnp.float32), axis=-1).astype(v.dtype)
        p_past = p[..., :n_sel * MOBA_BLOCK].reshape(b, h, MOBA_QCHUNK, n_sel, MOBA_BLOCK)
        p_own = p[..., n_sel * MOBA_BLOCK:]
        return (jnp.einsum('bhqks,bhqksd->bhqd', p_past, v_sel)
                + jnp.einsum('bhqs,bhsd->bhqd', p_own, v_own))

    out = lax.map(chunk, jnp.arange(t // MOBA_QCHUNK))
    return out.transpose(1, 0, 3, 2, 4).reshape(b, t, h * dh)

def _dsa_attention(q_lat, ckv, iq, ik, iw):
    b, t, h, c = q_lat.shape
    k_top = min(DSA_TOPK_MAX, t // 4)
    scale = DSA_HEAD_DIM ** -0.5
    bi = jnp.arange(b)[:, None, None]
    kpos = jnp.arange(t)

    def chunk(ci):
        t0 = ci * DSA_QCHUNK
        qpos = t0 + jnp.arange(DSA_QCHUNK)
        iq_c = lax.dynamic_slice_in_dim(iq, t0, DSA_QCHUNK, axis=1)
        iw_c = lax.dynamic_slice_in_dim(iw, t0, DSA_QCHUNK, axis=1)
        ql_c = lax.dynamic_slice_in_dim(q_lat, t0, DSA_QCHUNK, axis=1)
        idx = jnp.einsum('bqhd,bsd->bqhs', iq_c, ik)
        score = jnp.einsum('bqhs,bqh->bqs', jax.nn.relu(idx), iw_c)
        score = jnp.where(kpos[None, :] <= qpos[:, None], score, -jnp.inf)
        sel = lax.top_k(score, k_top)[1]
        kv = ckv[bi, sel]
        s = jnp.einsum('bqhc,bqkc->bqhk', ql_c, kv) * scale
        s = jnp.where((sel <= qpos[None, :, None])[:, :, None, :], s, -jnp.inf)
        p = jax.nn.softmax(s.astype(jnp.float32), axis=-1).astype(kv.dtype)
        return jnp.einsum('bqhk,bqkc->bqhc', p, kv)

    out = lax.map(chunk, jnp.arange(t // DSA_QCHUNK))
    return out.transpose(1, 0, 2, 3, 4).reshape(b, t, h, c)

def _even_layer(x, norm_g, w_in, b_glu, w_dw, b_dw, ln_g, ln_b, w_pw, b_pw, w_out):
    b, t, _ = x.shape
    z = _rmsnorm(x, norm_g) @ w_in
    a_val, a_gt, a_gate, q, k, v, b_gate = _split_cols(
        z, [CONV_WIDTH, CONV_WIDTH, CONV_WIDTH, MOBA_WIDTH, MOBA_WIDTH, MOBA_WIDTH, MOBA_WIDTH])
    ya = _conformer_conv(a_val + b_glu[:CONV_WIDTH], a_gt + b_glu[CONV_WIDTH:],
                         w_dw, b_dw, ln_g, ln_b, w_pw, b_pw) * jax.nn.silu(a_gate)
    shp = (b, t, MOBA_HEADS, MOBA_HEAD_DIM)
    yb = _moba_attention(q.reshape(shp), k.reshape(shp), v.reshape(shp)) * jax.nn.silu(b_gate)
    return jnp.concatenate([ya, yb], axis=-1) @ w_out

def _odd_layer(x, norm_g, w_in, q_norm, w_qb, kv_norm, w_uk, w_uv, w_iq, ik_g, ik_b, w_out):
    b, t, _ = x.shape
    z = _rmsnorm(x, norm_g) @ w_in
    cq, ckv, ik, iw, gate = _split_cols(z, [Q_LORA, KV_LORA, IDX_DIM, IDX_HEADS, DSA_WIDTH])
    cq = _rmsnorm(cq, q_norm)
    q = (cq @ w_qb).reshape(b, t, DSA_HEADS, DSA_HEAD_DIM)
    q_lat = jnp.einsum('bthd,hdc->bthc', q, w_uk)
    ckv = _rmsnorm(ckv, kv_norm)
    iq = (cq @ w_iq).reshape(b, t, IDX_HEADS, IDX_DIM)
    ik = _layernorm(ik, ik_g, ik_b)
    iw = iw * (IDX_HEADS ** -0.5 * IDX_DIM ** -0.5)
    o_lat = _dsa_attention(q_lat, ckv, iq, ik, iw)
    o = jnp.einsum('bthc,hcd->bthd', o_lat, w_uv).reshape(b, t, DSA_WIDTH)
    return (o * jax.nn.silu(gate)) @ w_out

def first_inputs(seed: int = 0) -> dict:
    key = jax.random.key(seed)
    ks = jax.random.split(key, 24)
    f32 = jnp.float32
    out_mult = (2.0 * DEPTH) ** -0.5

    def w(k, shape, fan_in, mult=1.0):
        return jax.random.normal(k, shape, f32) * (mult * fan_in ** -0.5)

    def gain(k, shape):
        return 1.0 + 0.02 * jax.random.normal(k, shape, f32)

    def bias(k, shape):
        return 0.02 * jax.random.normal(k, shape, f32)

    return {
        'x': jax.random.normal(ks[0], (BATCH, SEQ, D_MODEL), f32),
        'even_norm': gain(ks[1], (N_EVEN, D_MODEL)),
        'even_w_in': w(ks[2], (N_EVEN, D_MODEL, EVEN_IN), D_MODEL),
        'even_b_glu': bias(ks[3], (N_EVEN, 2 * CONV_WIDTH)),
        'even_w_dw': w(ks[4], (N_EVEN, CONV_KERNEL, CONV_WIDTH), CONV_KERNEL),
        'even_b_dw': bias(ks[5], (N_EVEN, CONV_WIDTH)),
        'even_conv_ln_g': gain(ks[6], (N_EVEN, CONV_WIDTH)),
        'even_conv_ln_b': bias(ks[7], (N_EVEN, CONV_WIDTH)),
        'even_w_pw': w(ks[8], (N_EVEN, CONV_WIDTH, CONV_WIDTH), CONV_WIDTH),
        'even_b_pw': bias(ks[9], (N_EVEN, CONV_WIDTH)),
        'even_w_out': w(ks[10], (N_EVEN, MIX_WIDTH, D_MODEL), MIX_WIDTH, out_mult),
        'odd_norm': gain(ks[11], (N_ODD, D_MODEL)),
        'odd_w_in': w(ks[12], (N_ODD, D_MODEL, ODD_IN), D_MODEL),
        'odd_q_norm': gain(ks[13], (N_ODD, Q_LORA)),
        'odd_w_qb': w(ks[14], (N_ODD, Q_LORA, DSA_WIDTH), Q_LORA),
        'odd_kv_norm': gain(ks[15], (N_ODD, KV_LORA)),
        'odd_w_uk': w(ks[16], (N_ODD, DSA_HEADS, DSA_HEAD_DIM, KV_LORA), DSA_HEAD_DIM),
        'odd_w_uv': w(ks[17], (N_ODD, DSA_HEADS, KV_LORA, DSA_HEAD_DIM), KV_LORA),
        'odd_w_iq': w(ks[18], (N_ODD, Q_LORA, IDX_HEADS * IDX_DIM), Q_LORA),
        'odd_ik_ln_g': gain(ks[19], (N_ODD, IDX_DIM)),
        'odd_ik_ln_b': bias(ks[20], (N_ODD, IDX_DIM)),
        'odd_w_out': w(ks[21], (N_ODD, DSA_WIDTH, D_MODEL), DSA_WIDTH, out_mult),
        'final_norm': gain(ks[22], (D_MODEL,)),
    }

def first_block(x, even_norm, even_w_in, even_b_glu, even_w_dw, even_b_dw, even_conv_ln_g,
              even_conv_ln_b, even_w_pw, even_b_pw, even_w_out, odd_norm, odd_w_in, odd_q_norm,
              odd_w_qb, odd_kv_norm, odd_w_uk, odd_w_uv, odd_w_iq, odd_ik_ln_g, odd_ik_ln_b,
              odd_w_out, final_norm):
    for layer in range(DEPTH):
        i = layer // 2
        if layer % 2 == 0:
            x = x + _even_layer(x, even_norm[i], even_w_in[i], even_b_glu[i], even_w_dw[i],
                                even_b_dw[i], even_conv_ln_g[i], even_conv_ln_b[i],
                                even_w_pw[i], even_b_pw[i], even_w_out[i])
        else:
            x = x + _odd_layer(x, odd_norm[i], odd_w_in[i], odd_q_norm[i], odd_w_qb[i],
                               odd_kv_norm[i], odd_w_uk[i], odd_w_uv[i], odd_w_iq[i],
                               odd_ik_ln_g[i], odd_ik_ln_b[i], odd_w_out[i])
    return _rmsnorm(x, final_norm)


CHUNK = 64
N_MIXERS = 3
DA_HEAD_DIM = 128
DA_HEADS = D_MODEL // (2 * DA_HEAD_DIM)
DA_VALUE_DIM = 2 * DA_HEAD_DIM
Q_BLOCK = 128
S5_GROUP = 16
S5_GROUPS = D_MODEL // S5_GROUP
S5_STATE = 64
S5_DT_MIN = 0.001
S5_DT_MAX = 0.1
RET_QK_DIM = 256
RET_HEADS = D_MODEL // RET_QK_DIM
RET_V_DIM = 2 * RET_QK_DIM
ROPE_BASE = 10000.0
D_FF = 4 * D_MODEL
N_A = (DEPTH + N_MIXERS - 1) // N_MIXERS
N_B = (DEPTH + N_MIXERS - 2) // N_MIXERS
N_C = DEPTH // N_MIXERS


F32 = jnp.float32

def rmsnorm(x, g):
    xf = x.astype(F32)
    y = xf * lax.rsqrt(jnp.mean(xf * xf, axis=-1, keepdims=True) + EPS)
    return (y * g.astype(F32)).astype(x.dtype)

def rotary(t, pos):
    half = t.shape[-1] // 2
    inv = 1.0 / (ROPE_BASE ** jnp.linspace(0.0, 1.0, half, dtype=F32))
    ang = pos[:, None] * inv[None, :]
    cos = jnp.cos(ang)[None, :, None, :]
    sin = jnp.sin(ang)[None, :, None, :]
    t1, t2 = t[..., :half], t[..., half:]
    return jnp.concatenate([t1 * cos - t2 * sin, t1 * sin + t2 * cos], axis=-1)

def diff_attention(h, w_in, lam_p, subln_g, w_out, lambda_init):
    B, S, D = h.shape
    q, k, v = jnp.split(h @ w_in, 3, axis=-1)
    q = q.reshape(B, S, DA_HEADS, 2, DA_HEAD_DIM).astype(F32) * DA_HEAD_DIM ** -0.5
    k = k.reshape(B, S, DA_HEADS, 2, DA_HEAD_DIM).astype(F32)
    v = v.reshape(B, S, DA_HEADS, DA_VALUE_DIM).astype(F32)
    lp = lam_p.astype(F32)
    lam = jnp.exp(jnp.sum(lp[0] * lp[1])) - jnp.exp(jnp.sum(lp[2] * lp[3])) + lambda_init
    n_blk = S // Q_BLOCK
    k_chunk = jnp.arange(S) // CHUNK
    q_blocks = q.reshape(B, n_blk, Q_BLOCK, DA_HEADS, 2, DA_HEAD_DIM).swapaxes(0, 1)

    def block(args):
        qb, bi = args
        q_chunk = (bi * Q_BLOCK + jnp.arange(Q_BLOCK)) // CHUNK
        mask = k_chunk[None, :] <= q_chunk[:, None]
        s = jnp.einsum('bqhtd,bkhtd->bhtqk', qb, k)
        p = jax.nn.softmax(jnp.where(mask, s, -jnp.inf), axis=-1)
        pd = p[:, :, 0] - lam * p[:, :, 1]
        return jnp.einsum('bhqk,bkhe->bqhe', pd, v)

    o = lax.map(block, (q_blocks, jnp.arange(n_blk)))
    o = o.swapaxes(0, 1).reshape(B, S, DA_HEADS, DA_VALUE_DIM)
    o = o * lax.rsqrt(jnp.mean(o * o, axis=-1, keepdims=True) + EPS)
    o = o * subln_g.astype(F32) * (1.0 - lambda_init)
    return o.reshape(B, S, D).astype(h.dtype) @ w_out

def _scan_combine(first, second):
    a1r, a1i, b1r, b1i = first
    a2r, a2i, b2r, b2i = second
    ar = a2r * a1r - a2i * a1i
    ai = a2r * a1i + a2i * a1r
    br = a2r * b1r - a2i * b1i + b2r
    bi = a2r * b1i + a2i * b1r + b2i
    return (ar, ai, br, bi)

def s5_mixer(h, a_re, a_im, log_dt, b_re, b_im, c_re, c_im, d_skip, w_glu):
    B, S, D = h.shape
    lam_re = a_re.astype(F32)
    lam_im = a_im.astype(F32)
    dt = jnp.exp(log_dt.astype(F32))[:, None]
    mag = jnp.exp(lam_re * dt)
    ab_re = mag * jnp.cos(lam_im * dt)
    ab_im = mag * jnp.sin(lam_im * dt)
    den = lam_re * lam_re + lam_im * lam_im
    nr, ni = ab_re - 1.0, ab_im
    coef_re = (nr * lam_re + ni * lam_im) / den
    coef_im = (ni * lam_re - nr * lam_im) / den
    br, bim = b_re.astype(F32), b_im.astype(F32)
    bb_re = coef_re[..., None] * br - coef_im[..., None] * bim
    bb_im = coef_re[..., None] * bim + coef_im[..., None] * br
    cr, ci = c_re.astype(F32), c_im.astype(F32)
    a_seq_re = jnp.broadcast_to(ab_re, (S, S5_GROUPS, S5_STATE))
    a_seq_im = jnp.broadcast_to(ab_im, (S, S5_GROUPS, S5_STATE))
    u = h.astype(F32).reshape(B, S, S5_GROUPS, S5_GROUP)

    def per_sequence(u_s):
        bu_re = jnp.einsum('sgc,gpc->sgp', u_s, bb_re)
        bu_im = jnp.einsum('sgc,gpc->sgp', u_s, bb_im)
        _, _, x_re, x_im = lax.associative_scan(
            _scan_combine, (a_seq_re, a_seq_im, bu_re, bu_im), axis=0)
        return jnp.einsum('sgp,gcp->sgc', x_re, cr) - jnp.einsum('sgp,gcp->sgc', x_im, ci)

    y = lax.map(per_sequence, u).reshape(B, S, D)
    y = y + d_skip.astype(F32) * h.astype(F32)
    g = jax.nn.gelu(y).astype(h.dtype)
    val, gate = jnp.split(g @ w_glu, 2, axis=-1)
    return val * jax.nn.sigmoid(gate)

def retention_mixer(h, w_in, w_out):
    B, S, D = h.shape
    proj = h @ w_in
    q, k, v, g = jnp.split(proj, [D, 2 * D, 4 * D], axis=-1)
    pos = jnp.arange(S, dtype=F32)
    q = rotary(q.reshape(B, S, RET_HEADS, RET_QK_DIM).astype(F32), pos)
    k = rotary(k.reshape(B, S, RET_HEADS, RET_QK_DIM).astype(F32), pos) * RET_QK_DIM ** -0.5
    v = v.reshape(B, S, RET_HEADS, RET_V_DIM).astype(F32)
    log_gamma = jnp.log(1.0 - jnp.exp2(-5.0 - jnp.arange(RET_HEADS, dtype=F32)))
    idx = jnp.arange(CHUNK, dtype=F32)
    intra_decay = jnp.exp(log_gamma[:, None, None] * jnp.abs(idx[:, None] - idx[None, :]))
    q_decay = jnp.exp(log_gamma[None, :] * (idx[:, None] + 1.0))
    k_decay = jnp.exp(log_gamma[None, :] * (CHUNK - 1.0 - idx[:, None]))
    chunk_decay = jnp.exp(log_gamma * CHUNK)
    n_ch = S // CHUNK

    def to_chunks(t):
        return t.reshape(B, n_ch, CHUNK, *t.shape[2:]).swapaxes(0, 1)

    def step(R, inp):
        qc, kc, vc = inp
        s = jnp.einsum('bnhd,bmhd->bhnm', qc, kc) * intra_decay
        o = jnp.einsum('bhnm,bmhe->bnhe', s, vc)
        o = o + jnp.einsum('bnhd,bhde->bnhe', qc * q_decay[..., None], R)
        R = R * chunk_decay[None, :, None, None] + jnp.einsum(
            'bmhd,bmhe->bhde', kc * k_decay[..., None], vc)
        return R, o

    R0 = jnp.zeros((B, RET_HEADS, RET_QK_DIM, RET_V_DIM), F32)
    _, o = lax.scan(step, R0, (to_chunks(q), to_chunks(k), to_chunks(v)))
    o = o.swapaxes(0, 1).reshape(B, S, RET_HEADS, RET_V_DIM)
    o = o * lax.rsqrt(jnp.mean(o * o, axis=-1, keepdims=True) + EPS)
    o = (jax.nn.silu(g.astype(F32)) * o.reshape(B, S, RET_HEADS * RET_V_DIM)).astype(h.dtype)
    return o @ w_out

def sqrelu_mlp(h, w1, w2):
    a = jax.nn.relu(h @ w1)
    return (a * a) @ w2

def second_inputs(seed: int = 0) -> dict:
    key = jax.random.key(seed)
    ks = jax.random.split(key, 24)
    D = D_MODEL

    def w(k, shape, fan_in):
        return jax.random.normal(k, shape, F32) * fan_in ** -0.5

    def gain(k, shape):
        return 1.0 + 0.02 * jax.random.normal(k, shape, F32)

    G, P, C = S5_GROUPS, S5_STATE, S5_GROUP
    return {
        "x": jax.random.normal(ks[0], (BATCH, SEQ, D), F32),
        "norm_mix": gain(ks[1], (DEPTH, D)),
        "norm_mlp": gain(ks[2], (DEPTH, D)),
        "norm_final": gain(ks[3], (D,)),
        "a_w_in": w(ks[4], (N_A, D, 3 * D), D),
        "a_lambda": 0.1 * jax.random.normal(ks[5], (N_A, 4, DA_HEAD_DIM), F32),
        "a_subln": gain(ks[6], (N_A, DA_VALUE_DIM)),
        "a_w_out": w(ks[7], (N_A, D, D), D),
        "b_a_re": -0.5 + 0.01 * jax.random.normal(ks[8], (N_B, G, P), F32),
        "b_a_im": jnp.pi * jnp.arange(P, dtype=F32)[None, None, :]
                  + 0.01 * jax.random.normal(ks[9], (N_B, G, P), F32),
        "b_log_dt": jax.random.uniform(ks[10], (N_B, G), F32,
                                       math.log(S5_DT_MIN), math.log(S5_DT_MAX)),
        "b_b_re": w(ks[11], (N_B, G, P, C), 2 * C),
        "b_b_im": w(ks[12], (N_B, G, P, C), 2 * C),
        "b_c_re": w(ks[13], (N_B, G, C, P), 2 * P),
        "b_c_im": w(ks[14], (N_B, G, C, P), 2 * P),
        "b_d": jax.random.normal(ks[15], (N_B, D), F32),
        "b_w_glu": w(ks[16], (N_B, D, 2 * D), D),
        "c_w_in": w(ks[17], (N_C, D, 6 * D), D),
        "c_w_out": w(ks[18], (N_C, 2 * D, D), 2 * D),
        "mlp_w1": w(ks[19], (DEPTH, D, D_FF), D),
        "mlp_w2": w(ks[20], (DEPTH, D_FF, D), D_FF),
    }

def second_block(x, norm_mix, norm_mlp, norm_final, a_w_in, a_lambda, a_subln, a_w_out,
              b_a_re, b_a_im, b_log_dt, b_b_re, b_b_im, b_c_re, b_c_im, b_d, b_w_glu,
              c_w_in, c_w_out, mlp_w1, mlp_w2):
    for i in range(DEPTH):
        kind = i % N_MIXERS
        j = i // N_MIXERS
        h = rmsnorm(x, norm_mix[i])
        if kind == 0:
            lambda_init = 0.8 - 0.6 * math.exp(-0.3 * i)
            mix = diff_attention(h, a_w_in[j], a_lambda[j], a_subln[j], a_w_out[j], lambda_init)
        elif kind == 1:
            mix = s5_mixer(h, b_a_re[j], b_a_im[j], b_log_dt[j], b_b_re[j], b_b_im[j],
                           b_c_re[j], b_c_im[j], b_d[j], b_w_glu[j])
        else:
            mix = retention_mixer(h, c_w_in[j], c_w_out[j])
        x = x + mix
        x = x + sqrelu_mlp(rmsnorm(x, norm_mlp[i]), mlp_w1[i], mlp_w2[i])
    return rmsnorm(x, norm_final)


def setup_inputs(seed=0):
    out = dict(first_inputs(seed))
    for name, value in second_inputs(seed + 1).items():
        if name != "x":
            out[name + "_2"] = value
    return out


def reference(
    x, even_norm, even_w_in, even_b_glu, even_w_dw, even_b_dw, even_conv_ln_g, even_conv_ln_b,
    even_w_pw, even_b_pw, even_w_out, odd_norm, odd_w_in, odd_q_norm, odd_w_qb, odd_kv_norm,
    odd_w_uk, odd_w_uv, odd_w_iq, odd_ik_ln_g, odd_ik_ln_b, odd_w_out, final_norm, norm_mix_2,
    norm_mlp_2, norm_final_2, a_w_in_2, a_lambda_2, a_subln_2, a_w_out_2, b_a_re_2, b_a_im_2,
    b_log_dt_2, b_b_re_2, b_b_im_2, b_c_re_2, b_c_im_2, b_d_2, b_w_glu_2, c_w_in_2, c_w_out_2,
    mlp_w1_2, mlp_w2_2,
):
    x = first_block(
        x, even_norm, even_w_in, even_b_glu, even_w_dw, even_b_dw, even_conv_ln_g,
        even_conv_ln_b, even_w_pw, even_b_pw, even_w_out, odd_norm, odd_w_in, odd_q_norm,
        odd_w_qb, odd_kv_norm, odd_w_uk, odd_w_uv, odd_w_iq, odd_ik_ln_g, odd_ik_ln_b,
        odd_w_out, final_norm,
    )
    return second_block(
        x, norm_mix_2, norm_mlp_2, norm_final_2, a_w_in_2, a_lambda_2, a_subln_2, a_w_out_2,
        b_a_re_2, b_a_im_2, b_log_dt_2, b_b_re_2, b_b_im_2, b_c_re_2, b_c_im_2, b_d_2,
        b_w_glu_2, c_w_in_2, c_w_out_2, mlp_w1_2, mlp_w2_2,
    )


_drawn_inputs = setup_inputs


def setup_inputs(seed=0):
    import zlib

    import numpy as np

    out = dict(_drawn_inputs(seed))
    spreads = {}
    factors = {'even_norm': 6.215,
     'even_b_glu': 7.424,
     'even_b_dw': 4.061,
     'even_conv_ln_g': 6.694,
     'even_conv_ln_b': 7.648,
     'even_b_pw': 4.753,
     'odd_norm': 3.673,
     'odd_q_norm': 5.036,
     'odd_kv_norm': 8.0,
     'odd_ik_ln_g': 5.045,
     'odd_ik_ln_b': 5.931,
     'norm_mlp_2': 2.677,
     'norm_final_2': 7.773,
     'a_subln_2': 3.842,
     'b_a_re_2': 64.0,
     'b_a_im_2': 35.128,
     'b_log_dt_2': 40.256,
     'b_b_re_2': 49.576,
     'b_b_im_2': 49.48,
     'b_c_re_2': 50.024,
     'b_c_im_2': 48.88}
    for name, (base, spread) in spreads.items():
        noise = np.random.default_rng([zlib.crc32(name.encode()), seed]).standard_normal(out[name].shape)
        drawn = base * np.exp(spread * noise) if base else spread * noise
        out[name] = jnp.asarray(drawn.astype(out[name].dtype))
    for name, factor in factors.items():
        out[name] = (out[name] * factor).astype(out[name].dtype)
    return out
```

```python
from collections import deque
from contextlib import ExitStack
import math

import numpy as np
import concourse.bass as bass
from concourse import mybir

ALU = mybir.AluOpType
ACT = mybir.ActivationFunctionType
AX = mybir.AxisListType
F32 = mybir.dt.float32
F32R = mybir.dt.float32r
I32 = mybir.dt.int32

EPS = 1e-6
NEG = -3.0e38
NR = 4
RS = 4
D = 2048
KTOP = 64

COLS = {}
_n = 0
for _name, _w in (("even_norm", 16), ("b_glu", 16), ("w_dw", 248), ("b_dw", 8), ("ln_g", 8), ("ln_b", 8),
                  ("b_pw", 8), ("odd_norm", 16), ("q_norm", 4), ("ik_g", 1), ("ik_b", 1), ("norm_mix", 32),
                  ("norm_mlp", 32), ("subln", 2), ("lam", 4), ("b_d", 16), ("a_re", 64), ("a_im", 64),
                  ("log_dt", 64), ("final", 16)):
    COLS[_name] = _n
    _n += _w
NCOLS = _n
CONST = {"ident": (0, 128), "ones": (128, 128), "causal": (256, 384), "chunk": (640, 384), "iota": (1024, 256),
         "even": (1280, 1), "odd": (1281, 1)}
NCONST = 1282


class Prog:

    ENG = ("pe", "act", "dve", "pool", "sp")

    def __init__(self):
        self.q = {e: [] for e in self.ENG}
        self.count = {}
        self.seen = {e: {} for e in self.ENG}

    def wait(self, e, waits):
        need = {}
        stack = [waits]
        while stack:
            w = stack.pop()
            if w is None:
                continue
            if isinstance(w, tuple) and len(w) == 2 and isinstance(w[0], str):
                need[w[0]] = max(need.get(w[0], 0), w[1])
            else:
                stack.extend(w)
        for s, v in need.items():
            if self.seen[e].get(s, 0) < v:
                self.seen[e][s] = v
                self.q[e].append(("wait", s, v))

    def emit(self, e, waits, fn, sig=True):
        self.wait(e, waits)
        self.q[e].append(("op", fn, e if sig else None, 1))
        if sig:
            self.count[e] = self.count.get(e, 0) + 1
            return (e, self.count[e])
        return None

    def dma(self, e, waits, out, in_, sem):
        self.wait(e, waits)
        self.q[e].append(("op", lambda g: g.dma_start(out, in_), sem, 16))
        self.count[sem] = self.count.get(sem, 0) + 16
        return (sem, self.count[sem])

    def now(self, *engines):
        return [(e, self.count[e]) for e in engines if self.count.get(e, 0)]

    def play(self, e, eng, sems):
        for item in self.q[e]:
            if item[0] == "wait":
                eng.wait_ge(sems[item[1]], item[2])
            else:
                ins = item[1](eng)
                if item[2]:
                    ins.then_inc(sems[item[2]], item[3])


def build_program(nc, t):
    P = Prog()
    top = ExitStack()

    def sb(name, shape, dt=F32, ctx=top):
        return ctx.enter_context(nc.sbuf_tensor(name, shape, dt))

    RAW = sb("RAW", [128, NR, 2048])
    WH = sb("WH", [128, RS, 1024], F32R)
    WL = sb("WL", [128, RS, 1024], F32R)
    X = sb("X", [128, 2, D])
    A1h = sb("A1h", [128, 16, 256], F32R)
    A1l = sb("A1l", [128, 16, 256], F32R)
    CV = sb("CV", [128, NCOLS])
    CID = sb("CID", [128, 256])
    ST = sb("ST", [128, 64])
    NS = sb("NS", [128, 64])
    DG = sb("DG", [128, 256])
    RB = sb("RB", [128, 256])
    G = [top.enter_context(nc.psum_tensor(f"G{i}", [128, 512], F32)) for i in range(4)]
    TB = [top.enter_context(nc.psum_tensor(f"T{i}", [128, 512], F32)) for i in range(4)]
    IDENT = CID[:, 0:128]
    ONES = CID[:, 128:256]

    def col(name, i=0, n=1):
        return CV[:, COLS[name] + i:COLS[name] + i + n]

    def act(out, in_, func, waits, scale=1.0, bias=0.0, accum=None):
        if accum is None:
            return P.emit("act", waits, lambda g: g.activation(out, in_, func, scale=scale, bias=bias))
        return P.emit("act", waits, lambda g: g.activation(out, in_, func, scale=scale, bias=bias, accum_out=accum))

    def tt(out, a, b, op, waits, e="dve"):
        return P.emit(e, waits, lambda g: g.tensor_tensor(out, a, b, op))

    def ts(out, a, s1, s2, op0, op1=None, waits=(), e="dve"):
        if op1 is None:
            return P.emit(e, waits, lambda g: g.tensor_scalar(out, a, s1, None, op0))
        return P.emit(e, waits, lambda g: g.tensor_scalar(out, a, s1, s2, op0, op1))

    def stt(out, a, s, b, op0, op1, waits):
        return P.emit("dve", waits, lambda g: g.scalar_tensor_tensor(out=out, in0=a, scalar=s, in1=b, op0=op0, op1=op1))

    def vcopy(out, a, waits):
        return P.emit("dve", waits, lambda g: g.tensor_copy(out, a))

    def recip(out, a, waits):
        return P.emit("dve", waits, lambda g: g.reciprocal(out, a))

    def rmax(out, a, waits, negate=False):
        return P.emit("dve", waits, lambda g: g.tensor_reduce(out, a, AX.X, ALU.max, negate=negate))

    def mm(out, lhsT, rhs, start, stop, waits=(), sig=False):
        return P.emit("pe", waits, lambda g: g.matmul(out, lhsT, rhs, start=start, stop=stop, skip_group_check=True), sig)

    def tr(out, in_, waits=(), sig=False):
        return P.emit("pe", waits, lambda g: g.transpose(out, in_, IDENT), sig)

    def split(hi, lo, src, waits):
        a = act(hi, src, ACT.Copy, waits)
        return tt(lo, src, hi.bitcast(F32), ALU.subtract, [a, waits])

    bank_free = [None] * 4
    bank_live = [False] * 4
    bank_next = [0]

    def bank():
        i = bank_next[0] % 4
        bank_next[0] += 1
        assert not bank_live[i]
        bank_live[i] = True
        return i, TB[i], bank_free[i]

    def release(i, tok):
        bank_live[i] = False
        bank_free[i] = tok

    chunks = []

    def stream_gemm(tag, w, K, n0, N, first=0, split_=True):
        kts = K // 128
        v = w.rearrange("(k p) n -> p k n", p=128)
        for k0 in [(first + k) % kts for k in range(0, kts, 4)]:
            chunks.append((tag, v[:, k0:k0 + 4, n0:n0 + N], (4, N), split_))

    def stream_raw(tag, src, shape):
        chunks.append((tag, src, shape, False))

    we, wo = t["even_w_in"][0], t["odd_w_in"][0]
    C = {"val": 0, "gt": 1024, "ag": 2048, "q": 3072, "k": 4096, "v": 5120, "bg": 6144}
    for i in range(2):
        stream_gemm(f"gt{i}", we, 2048, C["gt"] + 512 * i, 512)
        stream_gemm(f"val{i}", we, 2048, C["val"] + 512 * i, 512)
    for i in range(2):
        for c in "qkv":
            stream_gemm(f"{c}{i}", we, 2048, C[c] + 512 * i, 512)
    for c in ("bg", "ag"):
        for i in range(2):
            stream_gemm(f"{c}{i}", we, 2048, C[c] + 512 * i, 512)
    for i in range(2):
        stream_gemm(f"pw{i}", t["even_w_pw"][0], 1024, 512 * i, 512)
    for i in range(4):
        stream_gemm(f"eo{i}", t["even_w_out"][0], 2048, 512 * i, 512, 8)
    stream_gemm("cq", wo, 2048, 0, 512)
    stream_gemm("ckv", wo, 2048, 512, 336)
    stream_gemm("gate0", wo, 2048, 848, 512)
    for i in range(2):
        stream_gemm(f"iq{i}", t["odd_w_iq"][0], 512, 512 * i, 512)
    for i in range(4):
        stream_gemm(f"qb{i}", t["odd_w_qb"][0], 512, 512 * i, 512)
    for i in range(1, 4):
        stream_gemm(f"gate{i}", wo, 2048, 848 + 512 * i, 512)
    for i in range(2):
        stream_raw(f"uk{i}", t["odd_w_uk"][0, 8 * i:8 * i + 8].rearrange("h d c -> d h c"), (8, 256))
        stream_raw(f"uv{i}", t["odd_w_uv"][0, 8 * i:8 * i + 8].rearrange("h (c p) d -> p (h c) d", p=128), (16, 128))
    for i in range(4):
        stream_gemm(f"oo{i}", t["odd_w_out"][0], 2048, 512 * i, 512)
    for i in range(4):
        for c in range(3):
            stream_gemm(f"a{'qkv'[c]}{i}", t["a_w_in_2"][0], 2048, 2048 * c + 512 * i, 512)
    for i in range(4):
        stream_gemm(f"ao{i}", t["a_w_out_2"][0], 2048, 512 * i, 512)

    def stream_mlp(l):
        w1, w2 = t["mlp_w1_2"][l], t["mlp_w2_2"][l]
        for s in range(9):
            if s < 8:
                for i in range(2):
                    stream_gemm(f"m{l}u{s}{i}", w1, 2048, 1024 * s + 512 * i, 512)
            if s > 0:
                for i in range(4):
                    stream_gemm(f"m{l}d{s - 1}{i}", w2[1024 * (s - 1):1024 * s], 1024, 512 * i, 512)

    stream_mlp(0)
    for i in range(4):
        stream_gemm(f"gl{i}", t["b_w_glu_2"][0], 2048, 512 * i, 512, split_=i > 0)
        stream_gemm(f"gg{i}", t["b_w_glu_2"][0], 2048, 2048 + 512 * i, 512)
    stream_mlp(1)

    arrive = [None] * len(chunks)
    slot = [None] * len(chunks)
    free_slots = deque((i, None) for i in range(NR))
    halves = [(c, h) for c, ch in enumerate(chunks) if ch[3] for h in range(2)]
    half_at = {ch: n for n, ch in enumerate(halves)}
    half_ready = [None] * len(halves)
    half_read = [None] * len(halves)
    state = {"dma": 0, "split": 0, "chunk": 0}

    def raw_view(c):
        a, b = chunks[c][2]
        return RAW[:, slot[c], 0:a * b].rearrange("p (a b) -> p a b", b=b)

    def issue_dmas(n=len(chunks)):
        while state["dma"] < n and free_slots:
            c = state["dma"]
            slot[c], read = free_slots.popleft()
            arrive[c] = P.dma("sp", read, raw_view(c), chunks[c][1], f"w{slot[c]}")
            state["dma"] += 1

    def split_next():
        n = state["split"]
        if n >= len(halves):
            return False
        c, h = halves[n]
        if arrive[c] is None or (n >= RS and half_read[n - RS] is None):
            return False
        N = chunks[c][2][1]
        src = RAW[:, slot[c], h * 2 * N:(h + 1) * 2 * N]
        hi, lo = WH[:, n % RS, 0:2 * N], WL[:, n % RS, 0:2 * N]
        old = half_read[n - RS] if n >= RS else None
        a = act(hi, src, ACT.Copy, [arrive[c], old])
        d = tt(lo, src, hi.bitcast(F32), ALU.subtract, [a, arrive[c], old])
        half_ready[n] = d
        state["split"] += 1
        if h == 1:
            free_slots.append((slot[c], d))
            issue_dmas()
        return True

    def pump_stream():
        while split_next():
            pass

    soon = deque()
    bg = deque()

    def pump_bg(n):
        for _ in range(min(n, len(bg))):
            bg.popleft()()

    def flush_bg():
        pump_bg(len(bg))

    pair_free = [[None, None], [None, None]]
    pair_next = [0]

    def gemm(tag, Ah, Al, kts, fm, evac, ready, steps=0, kready=None, first=0):
        pp = pair_next[0] % 2
        pair_next[0] += 1
        B = G[2 * pp:2 * pp + 2]
        last = [None, None]
        P.wait("pe", ready)
        P.wait("pe", pair_free[pp])
        seen = 0
        for k0 in [(first + k) % kts for k in range(0, kts, 4)]:
            c = state["chunk"]
            assert chunks[c][0] == tag, (chunks[c][0], tag)
            N = chunks[c][2][1]
            for h in range(2):
                pump_stream()
                n = half_at[(c, h)]
                assert half_ready[n] is not None
                P.wait("pe", half_ready[n])
                for j in range(2):
                    kt = k0 + 2 * h + j
                    begin = seen == 0
                    seen += 1
                    if kready is not None:
                        P.wait("pe", kready(kt))
                    hi = WH[:, n % RS, j * N:(j + 1) * N]
                    lo = WL[:, n % RS, j * N:(j + 1) * N]
                    end = seen == kts
                    if fm:
                        for s in range(4):
                            o = B[s // 2][:, 256 * (s % 2):256 * (s % 2) + 256]
                            ws = slice(128 * s, 128 * s + 128)
                            mm(o, hi[:, ws], Ah[:, kt, :], begin and s % 2 == 0, False)
                            mm(o, hi[:, ws], Al[:, kt, :], False, False)
                            last[s // 2] = mm(o, lo[:, ws], Ah[:, kt, :], False, end,
                                              sig=s == 3 or (end and s % 2 == 1))
                    else:
                        for i in range(2):
                            o = B[i][:, 0:N]
                            tk = slice(128 * i, 128 * i + 128)
                            mm(o, Ah[:, kt, tk], hi, begin, False)
                            mm(o, Ah[:, kt, tk], lo, False, False)
                            last[i] = mm(o, Al[:, kt, tk], hi, False, end, sig=i == 1 or end)
                half_read[n] = last[1]
                if soon and seen > 2:
                    soon.popleft()()
                pump_bg(steps)
            state["chunk"] += 1
        for i in range(2):
            o = B[i][:, :].rearrange("p (a b) -> p a b", b=256) if fm else B[i][:, 0:N]
            pair_free[pp][i] = evac(o, i, last[i])

    def raw_chunk(tag):
        c = state["chunk"]
        assert chunks[c][0] == tag, (chunks[c][0], tag)
        state["chunk"] += 1
        assert arrive[c] is not None
        return c, raw_view(c), arrive[c]

    def free_raw(c, tok):
        free_slots.append((slot[c], tok))
        issue_dmas()

    def phase():
        assert not bg
        pump_stream()
        tok = P.now("pe", "act", "dve", "pool")
        for e in ("act", "dve", "pool"):
            P.wait(e, tok)
        return tok

    def rsqrt_col(out, m, tmp, waits):
        a = act(tmp, m, ACT.Sqrt, waits)
        b = recip(out, tmp, [a])
        b = tt(tmp, out, out, ALU.mult, [b])
        b = tt(tmp, tmp, m, ALU.mult, [b])
        b = ts(tmp, tmp, -0.5, 1.5, ALU.mult, ALU.add, [b])
        return tt(out, out, tmp, ALU.mult, [b])

    def rms_stats(src, junk, n, waits, s=0):
        a = None
        for i in range(2):
            a = act(junk[:, i, :], src[:, i, :], ACT.Square, waits, accum=ST[:, s + i:s + i + 1])
        b = ts(ST[:, s + 2:s + 4], ST[:, s:s + 2], 1.0 / n, EPS, ALU.mult, ALU.add, [a])
        return rsqrt_col(ST[:, s + 4:s + 6], ST[:, s + 2:s + 4], ST[:, s:s + 2], [b])

    def transpose_scaled(src, kts, g, evac, waits):
        toks = []
        for k in range(0, kts, 2):
            n = min(2, kts - k)
            b, T, free = bank()
            for j in range(n):
                for i in range(2):
                    tok = tr(T[:, 256 * j + 128 * i:256 * j + 128 * i + 128], src[:, i, (k + j) * 128:(k + j) * 128 + 128],
                             [free, waits], sig=(j == n - 1 and i == 1))
            r = evac(k, T[:, 0:256 * n].rearrange("p (a b) -> p a b", b=256), n, tok)
            release(b, r)
            toks.append(r)
        return toks

    def to_A(Ah, Al, g, off=0):
        def ev(k, ap, n, tok):
            a = [act(Ah[:, off + k + j, :], ap[:, j, :], ACT.Copy, [tok], scale=g(k + j)) for j in range(n)]
            for j in range(n):
                d = stt(Al[:, off + k + j, :], ap[:, j, :], g(k + j), Ah[:, off + k + j, :].bitcast(F32),
                        ALU.mult, ALU.subtract, [a[-1], tok])
            return d
        return ev

    x_tok = [{}, {}]
    nrm = {"n": 0}

    def x_done():
        return [v for d_ in x_tok for v in d_.values()]

    def norm_steps(blk, ev, old=None):
        n0 = 512 * blk
        w = [x_tok[0][n0], x_tok[1][n0]]

        def squares():
            for i in range(2):
                b, T, free = bank()
                r = act(T[:, 0:512], X[:, i, n0:n0 + 512], ACT.Square, [w, free, old],
                        accum=NS[:, 4 * i + blk:4 * i + blk + 1])
                release(b, r)
                nrm["sq", i, blk] = r

        def turn(k):
            def run():
                b, T, free = bank()
                for j in range(2):
                    for i in range(2):
                        c = 128 * (4 * blk + k + j)
                        tok = tr(T[:, 256 * j + 128 * i:256 * j + 128 * i + 128], X[:, i, c:c + 128], [free, w],
                                 sig=j == 1 and i == 1)
                r = ev(4 * blk + k, T[:, 0:512].rearrange("p (a b) -> p a b", b=256), 2, tok)
                release(b, r)
                for j in range(2):
                    nrm["k", 4 * blk + k + j] = r
            return run

        return [squares] + ([turn(0), turn(2)] if ev is not None else [])

    def row_scales(cols_tok, rcol):
        b, T, free = bank()
        r = None
        for i in range(2):
            r = ts(DG[:, 128 * i:128 * i + 128], IDENT, rcol[:, i:i + 1], None, ALU.mult, waits=[cols_tok, nrm.get("dg")])
        for i in range(2):
            tk = mm(T[:, 128 * i:128 * i + 128], ONES, DG[:, 128 * i:128 * i + 128], True, True, [free, r], sig=i == 1)
        nrm["dg"] = tk
        r = vcopy(RB[:, :], T[:, 0:256], [tk])
        release(b, r)
        return r

    def norm_finish(rows=True, waits=()):
        sq = [nrm["sq", i, k] for i in range(2) for k in range(4)]
        S_ = NS[:, 0:8].rearrange("p (a b) -> p a b", b=4)
        r = P.emit("dve", [sq, waits], lambda g: g.tensor_reduce(NS[:, 8:10], S_, AX.X, ALU.add))
        r = ts(NS[:, 8:10], NS[:, 8:10], 1.0 / D, EPS, ALU.mult, ALU.add, [r])
        r = rsqrt_col(NS[:, 12:14], NS[:, 8:10], NS[:, 10:12], [r])
        r = tt(NS[:, 14:16], NS[:, 12:14], NS[:, 12:14], ALU.mult, [r])
        nrm["r"] = r
        if rows:
            rows_soon()
        return r

    def rows_soon():
        def run():
            nrm["rb"] = row_scales(nrm["r"], NS[:, 12:14])
        soon.append(run)

    RC = [NS[:, 12:13], NS[:, 13:14]]
    R2 = [NS[:, 14:15], NS[:, 15:16]]
    RB2 = RB[:, :].unsqueeze(1).to_broadcast([128, 2, 256])

    def kA(kt):
        return nrm["k", kt]

    def accumulate(n0, ev=None, scale=None, last=True, old=None, then=()):
        def run(ap, i, tok):
            xs = X[:, i, n0:n0 + 512]
            if scale is None:
                r = tt(xs, xs, ap, ALU.add, [tok, x_tok[i].get(n0)])
            else:
                r = stt(xs, ap, scale[i], xs, ALU.mult, ALU.add, [tok, x_tok[i].get(n0), nrm["r"]])
            x_tok[i][n0] = r
            if last and i == 1:
                bg.extend(norm_steps(n0 // 512, ev, old) + list(then))
            return r
        return run

    def softmax(S, p, mask, scale, st, tok, extra=()):
        a = stt(p, S[:, 0:384], scale, mask, ALU.mult, ALU.add, [tok, extra])
        free = a
        m = [rmax(ST[:, st + i:st + i + 1], p[:, (0, 128)[i]:(128, 384)[i]], [a], negate=True) for i in range(2)]
        for i in range(2):
            v = p[:, (0, 128)[i]:(128, 384)[i]]
            e = act(v, v, ACT.Exp, [m[i]], bias=ST[:, st + i:st + i + 1], accum=ST[:, st + 2 + i:st + 3 + i])
        r = recip(ST[:, st + 4:st + 6], ST[:, st + 2:st + 4], [e])
        for i in range(2):
            v = p[:, (0, 128)[i]:(128, 384)[i]]
            d = ts(v, v, ST[:, st + 4 + i:st + 5 + i], None, ALU.mult, waits=[r])
        return free, d

    def transpose_p(p, tok):
        b, T, free = bank()
        tr(T[:, 0:128], p[:, 0:128], [free, tok])
        tr(T[:, 128:256], p[:, 128:256])
        tk = tr(T[:, 256:384], p[:, 256:384], sig=True)
        return b, T, tk

    c1 = P.dma("act", None, CID[:, :], t["consts"][:, 0:256], "m_id")
    c0 = P.dma("act", None, CV[:, :], t["cols"], "m_cv")
    xv = t["x"][0].rearrange("(i p) n -> p i n", p=128)
    for k in range(4):
        r = P.dma("sp", None, X[:, :, 512 * k:512 * k + 512], xv[:, :, 512 * k:512 * k + 512], f"m_x{k}")
        x_tok[0][512 * k] = x_tok[1][512 * k] = [r, c1]
        if k < 2:
            issue_dmas(k + 1)
    issue_dmas()
    P.wait("act", c0)
    P.wait("dve", c0)
    ns = [norm_steps(k, to_A(A1h, A1l, lambda k_: col("even_norm", k_)), c1) for k in range(4)]
    for k in range(2):
        for st in ns[k][1:]:
            st()
        split_next()
        split_next()

    def first_rows():
        nrm["rb"] = row_scales(nrm["r"], NS[:, 12:14])

    bg.extend([ns[0][0], lambda: None, ns[1][0], ns[2][1], ns[2][2], ns[3][1], ns[3][2], ns[2][0], ns[3][0],
               lambda: norm_finish(rows=False), first_rows])

    ctx = ExitStack()
    A2h = sb("A2h_e", [128, 16, 256], F32R, ctx)
    A2l = sb("A2l_e", [128, 16, 256], F32R, ctx)
    MK = sb("MK_e", [128, 384], ctx=ctx)
    U = sb("U", [128, 8, 286], ctx=ctx)
    Y = sb("Y", [128, 8, 256], ctx=ctx)
    BG = sb("BG", [128, 8, 256], ctx=ctx)
    SC = sb("SC_e", [128, 4, 384], ctx=ctx)
    ctxq = ExitStack()
    QT = sb("QT", [128, 8, 256], ctx=ctxq)
    KT = sb("KT", [128, 8, 256], ctx=ctxq)
    V = sb("V", [128, 2, 1024], ctx=ctxq)
    SG = SC[:, :, :].rearrange("p a b -> p (a b)")[:, 0:1024].rearrange("p (a b) -> p a b", b=256)
    mk = P.dma("pool", None, MK[:, :], t["consts"][:, 256:640], "m_mk")
    z = P.emit("pool", None, lambda g: g.memset(U[:, :, 0:30], 0.0))
    sg_read = [None] * 2
    u_tok = [None] * 8

    def ev_gt(nb):
        def ev(ap, i, tok):
            g = SG[:, 2 * i:2 * i + 2, :]
            r = tt(g, ap, RB2, ALU.mult, [tok, sg_read[i], nrm["rb"]])
            for j in range(2):
                s = 2 * i + j
                sg_tok[i] = act(SG[:, s, :], SG[:, s, :], ACT.Sigmoid, [r], bias=col("b_glu", 8 + 4 * nb + s))
            return r
        return ev

    def ev_val(nb):
        def ev(ap, i, tok):
            c = 4 * nb + 2 * i
            f = tt(U[:, c:c + 2, 30:286], ap, RB2, ALU.mult, [tok, nrm["rb"]])
            for j in range(2):
                r = stt(U[:, c + j, 30:286], U[:, c + j, 30:286], col("b_glu", c + j), SG[:, 2 * i + j, :],
                        ALU.add, ALU.mult, [f, sg_tok[i]])
                u_tok[c + j] = r
            sg_read[i] = r
            return f
        return ev

    sg_tok = [None] * 2
    y_tok = [None] * 8

    def conv_step(j, c4):
        def run():
            for c in range(c4, c4 + 4):
                w = col("w_dw", 31 * c + j)
                if j == 0:
                    y_tok[c] = ts(Y[:, c, :], U[:, c, 0:256], w, col("b_dw", c), ALU.mult, ALU.add, [u_tok[c], z])
                else:
                    y_tok[c] = stt(Y[:, c, :], U[:, c, j:j + 256], w, Y[:, c, :], ALU.mult, ALU.add, [y_tok[c], z])
        return run

    for nb in range(2):
        gemm(f"gt{nb}", A1h, A1l, 16, True, ev_gt(nb), None, 1 if nb else 2, kready=kA)
        gemm(f"val{nb}", A1h, A1l, 16, True, ev_val(nb), None, nb)
        bg.extend(conv_step(j, 4 * nb) for j in range(31))

    def ev_fm(dst, c0_, func=None, out_tok=None, waits=None, rows=True):
        def ev(ap, i, tok):
            o = dst[:, c0_ + 2 * i:c0_ + 2 * i + 2, :]
            r = tt(o, ap, RB2, ALU.mult, [tok, waits, nrm["rb"]]) if rows else act(o, ap, ACT.Copy, [tok, waits])
            f = act(o, o, func, [r]) if func is not None else r
            if out_tok is not None:
                out_tok.append(f)
            return r
        return ev

    def ev_tm(dst, n0, N=512, out_tok=None):
        def ev(ap, i, tok):
            r = act(dst[:, i, n0:n0 + N], ap[:, 0:N], ACT.Copy, [tok, nrm["r"]], scale=RC[i])
            if out_tok is not None:
                out_tok.append(r)
            return r
        return ev

    qkv = []
    for i in range(2):
        gemm(f"q{i}", A1h, A1l, 16, True, ev_fm(QT, 4 * i, out_tok=qkv), None, 1)
        gemm(f"k{i}", A1h, A1l, 16, True, ev_fm(KT, 4 * i, out_tok=qkv), None, 1)
        gemm(f"v{i}", A1h, A1l, 16, False, ev_tm(V, 512 * i, out_tok=qkv), None, 1)
    bgt = []
    gemm("bg0", A1h, A1l, 16, True, ev_fm(BG, 0, ACT.Silu, bgt), None, 1)

    sc_free = [None] * 4
    yb = []

    def moba(h):
        n = h % 2
        p, pT = SC[:, n, :], SC[:, 2 + n, :]
        s = {}

        def scores():
            b, T, free = bank()
            mm(T[:, 0:128], QT[:, h, 0:128], KT[:, h, 0:128], True, True, [free, qkv])
            tk = mm(T[:, 128:384], QT[:, h, 128:256], KT[:, h, :], True, True, sig=True)
            f, s["p"] = softmax(T, p, MK[:, :], 128.0 ** -0.5, 8 + 8 * n, tk, [mk, sc_free[n], sg_read])
            release(b, f)

        def turn():
            b, T, tk = transpose_p(p, s["p"])
            sc_free[n] = tk
            s["pT"] = act(pT, T[:, 0:384], ACT.Copy, [tk, sc_free[2 + n], sg_read])
            release(b, s["pT"])

        def pv():
            b, T, free = bank()
            mm(T[:, 0:256], V[:, 0, 128 * h:128 * h + 128], pT[:, 0:256], True, False, [free, s["pT"]])
            tk = mm(T[:, 128:256], V[:, 1, 128 * h:128 * h + 128], pT[:, 256:384], False, True, sig=True)
            sc_free[2 + n] = tk
            g = tt(BG[:, h, :], T[:, 0:256], BG[:, h, :], ALU.mult, [tk, bgt])
            release(b, g)
            yb.append(split(A2h[:, 8 + h, :], A2l[:, 8 + h, :], BG[:, h, :], [g]))

        return [scores, turn, pv]

    ms = [moba(h) for h in range(8)]
    for h in range(9):
        if h < 8:
            bg.append(ms[h][0])
        if h > 0:
            bg.append(ms[h - 1][1])
            bg.append(ms[h - 1][2])
    gemm("bg1", A1h, A1l, 16, True, ev_fm(BG, 4, ACT.Silu, bgt), None, 1)
    GA = U[:, :, 0:256]
    ga = []

    def ev_ga(nb):
        def ev(ap, i, tok):
            o = GA[:, 4 * nb + 2 * i:4 * nb + 2 * i + 2, :]
            r = tt(o, ap, RB2, ALU.mult, [tok, y_tok])
            ga.append(act(o, o, ACT.Silu, [r]))
            return r
        return ev

    LN = SC[:, :, :].rearrange("p a b -> p (a b)")
    MU, VAR, RSD = LN[:, 0:256], LN[:, 256:512], LN[:, 512:768]
    ln = {}

    def ln_sum(src, w):
        b, T, free = bank()
        for c in range(8):
            tk = mm(T[:, 0:256], ONES, src[:, c, :], c == 0, c == 7, [free, w], sig=c == 7)
        return b, T, tk

    def ln_mean():
        b, T, tk = ln_sum(Y, y_tok)
        ln["mu"] = ts(MU, T[:, 0:256], 1.0 / 1024, None, ALU.mult, waits=[tk, yb, sc_free])
        release(b, ln["mu"])

    def ln_center(c):
        def run():
            d = tt(Y[:, c:c + 4, :], Y[:, c:c + 4, :], MU.unsqueeze(1).to_broadcast([128, 4, 256]), ALU.subtract, ln["mu"])
            ln["q", c] = act(BG[:, c:c + 4, :], Y[:, c:c + 4, :], ACT.Square, [d, yb])
        return run

    def ln_var():
        b, T, tk = ln_sum(BG, [ln["q", 0], ln["q", 4]])
        r = ts(VAR, T[:, 0:256], 1.0 / 1024, EPS, ALU.mult, ALU.add, [tk])
        release(b, r)
        ln["r"] = rsqrt_col(RSD, VAR, MU, [r])

    def ln_out(c):
        def run():
            d = tt(Y[:, c:c + 4, :], Y[:, c:c + 4, :], RSD.unsqueeze(1).to_broadcast([128, 4, 256]), ALU.mult, ln["r"])
            for k in range(c, c + 4):
                ln["y", k] = act(Y[:, k, :], Y[:, k, :], ACT.Silu, [d], scale=col("ln_g", k), bias=col("ln_b", k))
        return run

    gemm("ag0", A1h, A1l, 16, True, ev_ga(0), None, 2)
    flush_bg()
    heads_done = P.now("pe")
    ctxq.close()
    PWh = sb("PWh", [128, 8, 256], F32R, ctx)
    PWl = sb("PWl", [128, 8, 256], F32R, ctx)
    pwin = {}

    def ln_split(c):
        def run():
            for k in (c, c + 2):
                pwin[k // 2] = split(PWh[:, k:k + 2, :], PWl[:, k:k + 2, :], Y[:, k:k + 2, :],
                                     [ln["y", k], ln["y", k + 1], heads_done])
        return run

    bg.extend([ln_mean, ln_center(0), ln_center(4), ln_var, ln_out(0), ln_split(0), ln_out(4), ln_split(4)])
    gemm("ag1", A1h, A1l, 16, True, ev_ga(1), None, 1)
    flush_bg()
    ya = []

    def ev_pw(nb):
        def ev(ap, i, tok):
            for j in range(2):
                c = 4 * nb + 2 * i + j
                r = stt(GA[:, c, :], ap[:, j, :], col("b_pw", c), GA[:, c, :], ALU.add, ALU.mult, [tok, ga])
            c = 4 * nb + 2 * i
            ya.append(split(A2h[:, c:c + 2, :], A2l[:, c:c + 2, :], GA[:, c:c + 2, :], [r]))
            return r
        return ev

    for i in range(2):
        gemm(f"pw{i}", PWh, PWl, 8, True, ev_pw(i), None, kready=lambda kt: pwin[kt // 2])
    a1_free = P.now("pe")
    ev_odd = to_A(A1h, A1l, lambda k: col("odd_norm", k))
    for i in range(4):
        gemm(f"eo{i}", A2h, A2l, 16, False, accumulate(512 * i, ev_odd, old=a1_free), None, 1,
             kready=lambda kt: yb if kt >= 8 else ya, first=8)
    flush_bg()
    norm_finish()
    ctx.close()

    ph = phase()
    ctx = ExitStack()
    A2h = sb("A2h_o", [128, 16, 256], F32R, ctx)
    A2l = sb("A2l_o", [128, 16, 256], F32R, ctx)
    CKV = sb("CKV", [128, 2, 256], ctx=ctx)
    CKT = sb("CKT", [128, 2, 256], ctx=ctx)
    GT = sb("GT", [128, 16, 256], ctx=ctx)
    QT = sb("QT_o", [128, 16, 256], ctx=ctx)
    MM = sb("MM", [128, 384], ctx=ctx)
    MK = sb("MK_o", [128, 384], ctx=ctx)
    KG = sb("KG", [128, 256], ctx=ctx)
    Z = sb("Z", [128, 4416], ctx=ctx)
    mk = P.dma("pool", ph, MK[:, :], t["consts"][:, 256:640], "m_mk")
    kg = P.dma("pool", ph, KG[:, :], t["kv_row"], "m_kg")
    zoff = [0]

    def zv(*shape):
        n = int(np.prod(shape))
        v = Z[:, zoff[0]:zoff[0] + n]
        zoff[0] += n
        if len(shape) == 2:
            v = v.rearrange("p (a b) -> p a b", b=shape[1])
        return v

    CQ = zv(2, 512)
    IK = zv(2, 128)
    IKT = zv(256)
    IQ = zv(8, 256)
    IW = zv(2, 16)
    SCR = zv(384)
    RL = zv(2, 128)

    cqt = []
    gemm("cq", A1h, A1l, 16, False, ev_tm(CQ, 0, out_tok=cqt), None, kready=kA)
    iws = ts(NS[:, 16:18], NS[:, 12:14], 16.0 ** -0.5 * 64.0 ** -0.5, None, ALU.mult, waits=nrm["r"])
    ckt = []

    def ev_ckv(ap, i, tok):
        act(CKV[:, i, :], ap[:, 0:256], ACT.Copy, [tok], scale=RC[i])
        act(IK[:, i, 0:64], ap[:, 256:320], ACT.Copy, [tok], scale=RC[i])
        r = act(IW[:, i, :], ap[:, 320:336], ACT.Copy, [tok, iws], scale=NS[:, 16 + i:17 + i])
        ckt.append(r)
        return r

    gemm("ckv", A1h, A1l, 16, False, ev_ckv, None)
    cqT = []

    def prep_cq():
        r = rms_stats(CQ, QT[:, 0:4, :].rearrange("p (a b) c -> p a (b c)", a=2), 512, cqt)
        for i in range(2):
            r = ts(CQ[:, i, :], CQ[:, i, :], ST[:, 4 + i:5 + i], None, ALU.mult, waits=[r])
        ckr["cq"] = r

    def turn_cq():
        r = ckr["cq"]
        cqT.append(transpose_scaled(CQ, 4, None, to_A(A2h, A2l, lambda k: col("q_norm", k)), [r]))

    ckr = {}

    def prep_ckv():
        r = rms_stats(CKV, QT[:, 4:6, :], 256, ckt, s=8)
        for i in range(2):
            r = stt(CKV[:, i, :], CKV[:, i, :], ST[:, 12 + i:13 + i], KG[:, :], ALU.mult, ALU.mult, [r, kg])
        ckr["tm"] = r

    def turn_ckv():
        r = ckr["tm"]
        b, T, free = bank()
        for c in range(2):
            for i in range(2):
                tk = tr(T[:, 256 * c + 128 * i:256 * c + 128 * i + 128], CKV[:, i, 128 * c:128 * c + 128], [free, r],
                        sig=c == 1 and i == 1)
        r = act(CKT[:, :, :], T[:, :].rearrange("p (a b) -> p a b", b=256), ACT.Copy, [tk])
        release(b, r)
        ckr["fm"] = r

    def prep_ik():
        s = 16
        for i in range(2):
            a = act(RL[:, i, 0:64], IK[:, i, 0:64], ACT.Copy, ckt, accum=ST[:, s + i:s + i + 1])
        r = ts(ST[:, s:s + 2], ST[:, s:s + 2], -1.0 / 64, None, ALU.mult, waits=[a])
        for i in range(2):
            d = ts(IK[:, i, 0:64], IK[:, i, 0:64], ST[:, s + i:s + i + 1], None, ALU.add, waits=[r])
        for i in range(2):
            a = act(RL[:, i, 0:64], IK[:, i, 0:64], ACT.Square, [d], accum=ST[:, s + 2 + i:s + 3 + i])
        r = ts(ST[:, s + 2:s + 4], ST[:, s + 2:s + 4], 1.0 / 64, EPS, ALU.mult, ALU.add, [a])
        r = rsqrt_col(ST[:, s + 4:s + 6], ST[:, s + 2:s + 4], ST[:, s:s + 2], [r])
        for i in range(2):
            r = ts(IK[:, i, 0:64], IK[:, i, 0:64], ST[:, s + 4 + i:s + 5 + i], None, ALU.mult, waits=[r])
        ckr["ikt"] = vcopy(IK[:, :, 64:128], IK[:, :, 0:64], [r])

    def turn_ik():
        r = ckr["ikt"]
        b, T, free = bank()
        for i in range(2):
            tk = tr(T[:, 128 * i:128 * i + 128], IK[:, i, :], [free, r], sig=i == 1)
        r = act(IKT, T[:, 0:256], ACT.Identity, [tk], scale=col("ik_g"), bias=col("ik_b"))
        release(b, r)
        ckr["ik"] = r

    bg.extend([prep_cq, prep_ckv, turn_cq, prep_ik, turn_ckv, turn_ik])
    gts = []
    gemm("gate0", A1h, A1l, 16, True, ev_fm(GT, 0, ACT.Silu, gts), None, 1)
    flush_bg()
    iqt, qt = [], []
    for i in range(2):
        gemm(f"iq{i}", A2h, A2l, 4, True, ev_fm(IQ, 4 * i, out_tok=iqt, rows=False), cqT)

    sc_tok = [None]
    rl_read = [None, None]
    s_init = vcopy(SCR, MK[:, :], [mk, ckt])
    sc_tok[0] = s_init

    def index_head(h):
        def run():
            b, T, free = bank()
            r0 = 64 * (h % 2)
            l = IQ[r0:r0 + 64, h // 2, :]
            k = IKT[r0:r0 + 64, :]
            mm(T[:, 0:128], l[:, 0:128], k[:, 0:128], True, True, [free, iqt, ckr["ik"]])
            tk = mm(T[:, 128:384], l[:, 128:256], k, True, True, sig=True)
            rr = ts(T[:, 0:384], T[:, 0:384], 0.0, None, ALU.max, waits=[tk])
            r = stt(SCR[:, 0:128], T[:, 0:128], IW[:, 0, h:h + 1], SCR[:, 0:128], ALU.mult, ALU.add, [rr, sc_tok[0]])
            r = stt(SCR[:, 128:384], T[:, 128:384], IW[:, 1, h:h + 1], SCR[:, 128:384], ALU.mult, ALU.add,
                    [rr, sc_tok[0]])
            sc_tok[0] = r
            release(b, r)
        return run

    topk = {}

    def top_rows(i):
        c0_, c1_ = ((0, 128), (128, 384))[i]
        S = SCR[:, c0_:c1_]
        W = IQ[:, 2 * i:2 * i + 2, :].rearrange("p a b -> p (a b)")
        wk, eq = W[:, 0:c1_ - c0_], W[:, 256:256 + c1_ - c0_]
        M8 = ST[:, 32 + 8 * i:40 + 8 * i]
        cn = ST[:, 48 + 2 * i:49 + 2 * i]

        st = {}

        def eights(n0):
            def run():
                src, r = (wk, st["r"]) if n0 else (S, [sc_tok[0], iq_dead])
                for n in (n0, n0 + 1):
                    r = P.emit("dve", r, lambda g, s_=src: g.max(M8, s_))
                    if n < KTOP // 8 - 1:
                        r = P.emit("dve", r, lambda g, s_=src: g.match_replace(wk, M8, s_, NEG))
                        src = wk
                st["r"] = r
            return run

        def marks():
            r = st["r"]
            v = M8[:, 7:8]
            a = ts(wk, S, v, None, ALU.is_gt, waits=[r])
            r1 = P.emit("dve", [a], lambda g: g.tensor_reduce(cn, wk, AX.X, ALU.add))
            b_ = ts(eq, S, v, None, ALU.is_equal, waits=[r1])
            m = MM[:, c0_:c1_]
            sc = P.emit("dve", [b_], lambda g: g.tensor_tensor_scan(m, eq, eq, cn, ALU.bypass, ALU.add))
            topk[i] = (wk, eq, m, c0_, c1_, sc)

        return [eights(n) for n in range(0, KTOP // 8, 2)] + [marks]

    def top_rows2(i):
        def run():
            wk, eq, m, c0_, c1_, sc = topk[i]
            r = stt(m, m, float(KTOP) + 0.5, eq, ALU.is_lt, ALU.mult, [sc])
            r = tt(m, m, wk, ALU.max, [r])
            r = ts(m, m, -NEG, NEG, ALU.mult, ALU.add, [r])
            topk[i] = tt(m, m, MK[:, c0_:c1_], ALU.min, [r])
        return run

    bg.extend(index_head(h) for h in range(16))
    for i in range(4):
        gemm(f"qb{i}", A2h, A2l, 4, True, ev_fm(QT, 4 * i, out_tok=qt, rows=False), None, 3)
    flush_bg()
    iq_dead = P.now("pe")
    bg.extend(top_rows(0) + top_rows(1) + [top_rows2(0), top_rows2(1)])
    for i in range(1, 4):
        gemm(f"gate{i}", A1h, A1l, 16, True, ev_fm(GT, 4 * i, ACT.Silu, gts), None, 1)
    flush_bg()
    ph = phase()
    zoff[0] = 0
    QL = [zv(2, 256) for _ in range(2)]
    PP = [zv(384) for _ in range(2)]
    PT = [zv(384) for _ in range(2)]
    OL = [zv(2, 256) for _ in range(2)]
    fr = {}
    oo = []
    chunk_uk, chunk_uv = {}, {}

    def dsa(h):
        n = h % 2
        s = {}

        def scores():
            if h % 8 == 0:
                chunk_uk[h // 8] = raw_chunk(f"uk{h // 8}")
                chunk_uv[h // 8] = raw_chunk(f"uv{h // 8}")
            c, w, ar = chunk_uk[h // 8]
            b, T, free = bank()
            for j in range(2):
                tk = mm(T[:, 256 * j:256 * j + 256], w[:, h % 8, 128 * j:128 * j + 128], QT[:, h, :], True, True,
                        [free, ar, qt], sig=j == 1)
            if h % 8 == 7:
                free_raw(c, tk)
            r = act(QL[n], T[:, :].rearrange("p (a b) -> p a b", b=256), ACT.Copy, [tk, fr.get(("ql", n))])
            release(b, r)
            s["ql"] = r

        def soft():
            b, T, free = bank()
            q_ = QL[n]
            mm(T[:, 0:128], q_[:, 0, 0:128], CKT[:, 0, 0:128], True, False, [free, s["ql"]])
            mm(T[:, 0:128], q_[:, 1, 0:128], CKT[:, 1, 0:128], False, True)
            mm(T[:, 128:384], q_[:, 0, 128:256], CKT[:, 0, :], False, False)
            tk = mm(T[:, 128:384], q_[:, 1, 128:256], CKT[:, 1, :], False, True, sig=True)
            fr["ql", n] = tk
            f, s["p"] = softmax(T, PP[n], MM[:, :], 128.0 ** -0.5, 8 + 8 * n, tk, [fr.get(("p", n)), topk[0], topk[1]])
            release(b, f)

        def turn():
            b, T, tk = transpose_p(PP[n], s["p"])
            fr["p", n] = tk
            s["pT"] = act(PT[n], T[:, 0:384], ACT.Copy, [tk, fr.get(("pT", n))])
            release(b, s["pT"])

        def pv():
            b, T, free = bank()
            pT = PT[n]
            for j in range(2):
                o = T[:, 256 * j:256 * j + 256]
                mm(o, CKV[:, 0, 128 * j:128 * j + 128], pT[:, 0:256], j == 0, False, [free, s["pT"]])
                tk = mm(o[:, 128:256], CKV[:, 1, 128 * j:128 * j + 128], pT[:, 256:384], False, True, sig=j == 1)
            fr["pT", n] = tk
            s["ol"] = act(OL[n], T[:, :].rearrange("p (a b) -> p a b", b=256), ACT.Copy, [tk, fr.get(("ol", n))])
            release(b, s["ol"])

        def out():
            c, w, ar = chunk_uv[h // 8]
            b, T, free = bank()
            mm(T[:, 0:256], w[:, 2 * (h % 8), :], OL[n][:, 0, :], True, False, [free, ar, s["ol"]])
            tk = mm(T[:, 0:256], w[:, 2 * (h % 8) + 1, :], OL[n][:, 1, :], False, True, sig=True)
            fr["ol", n] = tk
            if h % 8 == 7:
                free_raw(c, tk)
            g = tt(GT[:, h, :], T[:, 0:256], GT[:, h, :], ALU.mult, [tk, gts])
            release(b, g)
            oo.append(split(A2h[:, h, :], A2l[:, h, :], GT[:, h, :], [g]))

        return [scores, soft, turn, pv, out]

    ds = [dsa(h) for h in range(16)]
    for rnd in range(16 + 4):
        for k in (4, 3, 2, 1, 0):
            h = rnd - k
            if 0 <= h < 16:
                if rnd < 16:
                    ds[h][k]()
                else:
                    bg.append(ds[h][k])
        if 9 <= rnd < 16:
            split_next()
    GP = NS[:, 32:48]
    gp = tt(GP, col("final", 0, 16), col("norm_mix", 0, 16), ALU.mult, None)
    ev_dif = to_A(A1h, A1l, lambda k: GP[:, k:k + 1])
    P.wait("act", gp)
    P.wait("dve", gp)
    a1_free = P.now("pe")
    for i in range(4):
        gemm(f"oo{i}", A2h, A2l, 16, False, accumulate(512 * i, ev_dif, old=[a1_free, gp]), None, 1 if i else 2,
             kready=lambda kt: oo[kt])
    flush_bg()
    r = norm_finish(rows=False)
    ctx.close()

    ph = phase()
    ctx = ExitStack()
    A2h = sb("A2h_a", [128, 16, 256], F32R, ctx)
    A2l = sb("A2l_a", [128, 16, 256], F32R, ctx)
    MK = sb("MK_a", [128, 384], ctx=ctx)
    Qb = [sb(f"Qa{i}", [128, 4, 256], ctx=ctx) for i in range(2)]
    Kb = [sb(f"Ka{i}", [128, 4, 256], ctx=ctx) for i in range(2)]
    Vb = [sb(f"Va{i}", [128, 2, 512], ctx=ctx) for i in range(2)]
    PA = [sb(f"PA{i}", [128, 2, 384], ctx=ctx) for i in range(2)]
    PTa = [sb(f"PTa{i}", [128, 384], ctx=ctx) for i in range(2)]
    OA = [sb(f"OA{i}", [128, 2, 256], ctx=ctx) for i in range(2)]
    JK = sb("JK", [128, 2, 256], ctx=ctx)
    GR = sb("GR", [128, D], ctx=ctx)
    ld = P.dma("act", ph, GR[:, :], t["final_row"], "m_row")
    r1 = vcopy(NS[:, 18:20], NS[:, 12:14], nrm["r"])
    turned = P.now("pe")

    def rescale(k):
        def run():
            for i in range(2):
                xs = X[:, i, 512 * k:512 * k + 512]
                x_tok[i][512 * k] = stt(xs, xs, NS[:, 18 + i:19 + i], GR[:, 512 * k:512 * k + 512], ALU.mult, ALU.mult,
                                        [r1, ld, x_tok[i][512 * k], turned])

        return run, lambda: norm_steps(k, None, None)[0]()

    def rescaled():
        r = norm_finish(rows=False)
        nrm["r"] = tt(NS[:, 12:14], NS[:, 12:14], NS[:, 18:20], ALU.mult, [r])

    def rescaled_rows():
        nrm["rb"] = row_scales(nrm["r"], NS[:, 12:14])

    mk = P.dma("pool", ph, MK[:, :], t["consts"][:, 640:1024], "m_mk")
    L = ST[:, 48:56]
    lam = []

    def lam_dots():
        r = tt(L[:, 0:1], col("lam", 0), col("lam", 1), ALU.mult, ph)
        lam.append(tt(L[:, 1:2], col("lam", 2), col("lam", 3), ALU.mult, [r]))

    def lam_exps():
        b, T, free = bank()
        tk = mm(T[:, 0:2], ONES, L[:, 0:2], True, True, [free, lam[0]], sig=True)
        r = act(L[:, 2:4], T[:, 0:2], ACT.Exp, [tk])
        release(b, r)
        r = tt(L[:, 4:5], L[:, 3:4], L[:, 2:3], ALU.subtract, [r])
        lam.append(ts(L[:, 5:6], L[:, 4:5], -lambda_init, None, ALU.add, waits=[r]))

    lambda_init = 0.8 - 0.6 * math.exp(-0.3 * 0)
    rs = [rescale(k) for k in range(4)]
    no = lambda: None
    bg.extend([lam_dots, no, rs[0][0], no] + [f for k in range(3) for f in (rs[k][1], rs[k + 1][0])]
              + [rs[3][1], lam_exps, rescaled, no, rescaled_rows])
    SUBG = ST[:, 56:58]
    sgt = ts(SUBG, col("subln", 0, 2), 1.0 - lambda_init, None, ALU.mult)
    fr = {}
    oo = []

    def diff(h, ready, done):
        n = h % 2
        s = {}
        Q_, K_, V_ = Qb[(h // 2) % 2], Kb[(h // 2) % 2], Vb[(h // 2) % 2]

        def scores(u):
            def run():
                b, T, free = bank()
                c = 2 * (h % 2) + u
                mm(T[:, 0:128], Q_[:, c, 0:128], K_[:, c, 0:128], True, True, [free, ready])
                tk = mm(T[:, 128:384], Q_[:, c, 128:256], K_[:, c, :], True, True, sig=True)
                f, s["p", u] = softmax(T, PA[n][:, u, :], MK[:, :], 128.0 ** -0.5, 8 + 8 * u, tk,
                                       [mk, fr.get(("p", n)), fr.get(("st", u))])
                fr["st", u] = s["p", u]
                release(b, f)
            return run

        def turn():
            d = stt(PA[n][:, 0, :], PA[n][:, 1, :], L[:, 5:6], PA[n][:, 0, :], ALU.mult, ALU.add,
                    [s["p", 0], s["p", 1], lam])
            b, T, tk = transpose_p(PA[n][:, 0, :], d)
            fr["p", n] = tk
            s["pT"] = act(PTa[n][:, :], T[:, 0:384], ACT.Copy, [tk, fr.get(("pT", n))])
            release(b, s["pT"])

        def pv():
            b, T, free = bank()
            pT = PTa[n]
            v0, v1 = (V_[:, i, 256 * (h % 2):256 * (h % 2) + 256] for i in range(2))
            mm(T[:, 0:256], pT[:, 0:128], v0, True, False, [free, s["pT"]])
            mm(T[:, 256:512], pT[:, 128:256], v0, False, False)
            tk = mm(T[:, 256:512], pT[:, 256:384], v1, False, True, sig=True)
            fr["pT", n] = tk
            done.append(tk)
            r = act(OA[n][:, :, :], T[:, :].rearrange("p (a b) -> p a b", b=256), ACT.Copy, [tk, fr.get(("o", n))])
            release(b, r)
            r = rms_stats(OA[n], JK, 256, [r, fr.get("rms")], s=24)
            for i in range(2):
                r = ts(OA[n][:, i, :], OA[n][:, i, :], ST[:, 28 + i:29 + i], None, ALU.mult, waits=[r])
            fr["rms"] = r
            s["o"] = r

        def out():
            tk = transpose_scaled(OA[n], 2, None, to_A(A2h, A2l, lambda k: SUBG[:, k:k + 1], off=2 * h), [s["o"], sgt])
            fr["o", n] = tk
            kt_tok[h] = tk

        return [scores(0), scores(1), turn, pv, out]

    done = [[], []]
    kt_tok = {}
    for i in range(4):
        rd = []
        w = done[i % 2]
        done[i % 2] = []
        Vd, Qd, Kd = Vb[i % 2], Qb[i % 2], Kb[i % 2]

        def ev_v(ap, k, tok):
            r = act(Vd[:, k, :], ap, ACT.Copy, [tok, w, nrm["r"]], scale=RC[k])
            rd.append(r)
            return r

        gemm(f"aq{i}", A1h, A1l, 16, True, ev_fm(Qd, 0, out_tok=rd, waits=w), None, 1 if i else 2, kready=kA)
        gemm(f"ak{i}", A1h, A1l, 16, True, ev_fm(Kd, 0, out_tok=rd, waits=w), None, 1)
        flush_bg()
        heads = [diff(h, rd, done[i % 2]) for h in (2 * i, 2 * i + 1)]
        bg.extend(st for hd in heads for st in hd[0:2])
        gemm(f"av{i}", A1h, A1l, 16, False, ev_v, None, 1)
        flush_bg()
        bg.extend(hd[k] for k in (2, 3, 4) for hd in heads)
    a1_free = P.now("pe")
    ev_mlp = to_A(A1h, A1l, lambda k: col("norm_mlp", k))
    for i in range(4):
        gemm(f"ao{i}", A2h, A2l, 16, False, accumulate(512 * i, ev_mlp, old=a1_free), None, 1,
             kready=lambda kt: kt_tok[kt // 2])
    flush_bg()
    norm_finish(rows=False)
    ctx.close()

    def mlp(l, Ah, Al, next_ev, ctx, side=(), then=((),) * 4):
        bg.extend(side)
        Bh = [sb(f"Bh{l}{i}", [128, 8, 256], F32R, ctx) for i in range(2)]
        Bl = [sb(f"Bl{l}{i}", [128, 8, 256], F32R, ctx) for i in range(2)]
        RE = [sb(f"RE{l}{i}", [128, 512], ctx=ctx) for i in range(2)]
        SQ = [sb(f"SQ{l}{i}", [128, 512], ctx=ctx) for i in range(2)]
        n_ev = [0]
        re_read, sq_read = [None, None], [None, None]
        b_read = [None, None]
        ready = [[], []]

        def ev_up(s, nb):
            def ev(ap, i, tok):
                n = n_ev[0] % 2
                n_ev[0] += 1
                R, S = (v[n][:, :].rearrange("p (a b) -> p a b", b=256) for v in (RE, SQ))
                a = act(R, ap, ACT.Relu, [tok, re_read[n]])
                d = stt(S, ap, 0.0, R, ALU.max, ALU.mult, [a, sq_read[n]])
                re_read[n] = d
                k = 4 * nb + 2 * i
                x_ = split(Bh[s % 2][:, k:k + 2, :], Bl[s % 2][:, k:k + 2, :], S, [d, b_read[s % 2]])
                sq_read[n] = x_
                ready[s % 2].append(x_)
                return d
            return ev

        for s in range(9):
            if s < 8:
                ready[s % 2] = []
                for i in range(2):
                    gemm(f"m{l}u{s}{i}", Ah, Al, 16, True, ev_up(s, i), None, 1, kready=kA)
            if s > 0:
                o = (s - 1) % 2
                if s == 8:
                    flush_bg()
                    old = P.now("pe")
                for i in range(4):
                    gemm(f"m{l}d{s - 1}{i}", Bh[o], Bl[o], 8, False,
                         accumulate(512 * i, next_ev, R2, s == 8, old if s == 8 else None, then[i]),
                         ready[o], 1)
                b_read[o] = P.now("pe")
        flush_bg()
        norm_finish(rows=next_ev is not None)

    MAGIC = 12582912.0
    ctxs = ExitStack()
    BD = [sb(f"BD{i}", [128, 64, 32], ctx=ctxs) for i in range(2)]
    CD = [sb(f"CD{i}", [128, 16, 128], ctx=ctxs) for i in range(2)]
    IO = sb("IO", [128, 258], ctx=ctxs)
    MAG = sb("MAG", [128, 64], ctx=ctxs)
    FQ = sb("FQ", [128, 64], ctx=ctxs)
    HT = sb("HT", [128, 16, 256], ctx=ctxs)
    ph = phase()
    HF = HT[:, :, :].rearrange("p a b -> p (a b)")
    BR = [HF[:, 1024 * i:1024 * i + 1024] for i in range(2)]
    T1, T2 = (HF[:, 2048 + 512 * i:2560 + 512 * i].rearrange("p (a b) -> p a b", b=16) for i in range(2))
    aw = [HF[:, 3072 + 64 * i:3136 + 64 * i] for i in range(12)]
    WI = HF[:, 3840:3904].bitcast(I32)
    io = P.dma("pool", ph, IO[:, :], t["consts"][:, 1024:1282], "m_io")
    ldb = [P.dma("pool", ph, BR[i], t["s5_b"][i], f"m_b{i}") for i in range(2)]
    z0 = [P.emit("pool", ph, lambda g, i=i: g.memset(BD[i][:, :, :], 0.0)) for i in range(2)]
    s5 = {}

    def exp_parts(z_, out1, outm1, waits, w):
        zc, k, kk, rr, p = w
        r = ts(zc, z_, -87.3, 88.0, ALU.max, ALU.min, waits)
        r = ts(k, zc, 1.4426950408889634, MAGIC, ALU.mult, ALU.add, [r])
        r = ts(k, k, -MAGIC, None, ALU.add, waits=[r])
        r = stt(rr, k, -0.693145751953125, zc, ALU.mult, ALU.add, [r])
        r = stt(rr, k, -1.4286068203094172e-06, rr, ALU.mult, ALU.add, [r])
        r = ts(p, rr, 1.0 / 40320, 1.0 / 5040, ALU.mult, ALU.add, [r])
        for f in (720, 120, 24, 6, 2, 1):
            r = tt(p, p, rr, ALU.mult, [r])
            r = ts(p, p, 1.0 / f, None, ALU.add, waits=[r])
            if f == 24:
                yield
        r = tt(p, p, rr, ALU.mult, [r])
        r = ts(WI, k, 127.0, 8388608.0, ALU.add, ALU.mult, [r])
        r = vcopy(kk, WI.bitcast(F32), [r])
        r = tt(p, p, kk, ALU.mult, [r])
        if outm1 is not None:
            r = ts(outm1, kk, -1.0, None, ALU.add, waits=[r])
            r = tt(outm1, outm1, p, ALU.add, [r])
        s5["r"] = tt(out1, p, kk, ALU.add, [r])
        yield

    def s5_params():
        LR, LI = col("a_re", 0, 64), col("a_im", 0, 64)
        dt_, th = aw[0], aw[1]
        yield from exp_parts(col("log_dt", 0, 64), dt_, None, None, aw[2:7])
        zr, em = aw[7], aw[8]
        r = tt(zr, LR, dt_, ALU.mult, [s5["r"]])
        yield from exp_parts(zr, MAG[:, :], em, [r], aw[2:7])
        r = tt(th, LI, dt_, ALU.mult, [s5["r"]])
        k, f = aw[2], aw[3]
        r = ts(k, th, 1.0 / (2 * math.pi), MAGIC, ALU.mult, ALU.add, [r])
        r = ts(k, k, -MAGIC, None, ALU.add, waits=[r])
        r = stt(f, k, -6.28125, th, ALU.mult, ALU.add, [r])
        r = stt(f, k, -0.0019350051879882812, f, ALU.mult, ALU.add, [r])
        r = stt(f, k, -3.019916050561733e-07, f, ALU.mult, ALU.add, [r])
        r = ts(f, f, 3.14159, -3.14159, ALU.min, ALU.max, [r])
        fq = ts(FQ[:, :], f, 1.0 / (2 * math.pi), None, ALU.mult, waits=[r])
        yield
        s1, s2 = aw[4], aw[5]
        act(s1, f, ACT.Sin, [fq])
        a = act(s2, f, ACT.Sin, [fq], scale=0.5)
        nr, ni, den, t1, cre, cim = aw[6], aw[7], aw[9], aw[10], aw[11], aw[3]
        r = tt(t1, s2, s2, ALU.mult, [a])
        r = tt(t1, t1, MAG[:, :], ALU.mult, [r])
        r = stt(nr, t1, -2.0, em, ALU.mult, ALU.add, [r])
        ni_t = tt(ni, MAG[:, :], s1, ALU.mult, [a])
        r = tt(den, LR, LR, ALU.mult, [r])
        q = tt(t1, LI, LI, ALU.mult, [r])
        r = tt(den, den, t1, ALU.add, [r, q])
        r = recip(den, den, [r])
        r = tt(cre, nr, LR, ALU.mult, [r])
        r = tt(t1, ni, LI, ALU.mult, [r, ni_t])
        r = tt(cre, cre, t1, ALU.add, [r])
        r = tt(cre, cre, den, ALU.mult, [r])
        yield
        r = tt(cim, ni, LR, ALU.mult, [r])
        r = tt(t1, nr, LI, ALU.mult, [r])
        r = tt(cim, cim, t1, ALU.subtract, [r])
        r = tt(cim, cim, den, ALU.mult, [r])
        B0, B1 = (b_.rearrange("p (a b) -> p a b", b=16) for b_ in BR)
        for i, (p_, q_, op) in enumerate(((B0, B1, ALU.subtract), (B1, B0, ALU.add))):
            for h in range(2):
                hs = slice(32 * h, 32 * h + 32)
                cr_, ci_ = (v[:, hs].unsqueeze(2).to_broadcast([128, 32, 16]) for v in (cre, cim))
                u = tt(T1, p_[:, hs, :], cr_, ALU.mult, [r, ldb])
                v = tt(T2, q_[:, hs, :], ci_, ALU.mult, [r, ldb])
                yield
                r = tt(BD[i][0:64, hs, 0:16], T1[0:64], T2[0:64], op, [u, v, z0])
                r = tt(BD[i][64:128, hs, 16:32], T1[64:128], T2[64:128], op, [u, v, z0])
        s5["bd"] = r
        ldc = [P.dma("pool", r, BR[i], t["s5_c"][i], f"m_c{i}") for i in range(2)]
        yield
        yield
        yield
        for i in range(2):
            for g_ in range(2):
                r = ts(CD[i][:, :, 64 * g_:64 * g_ + 64], BR[i].rearrange("p (a b) -> p a b", b=64),
                       IO[:, 256 + g_:257 + g_], 1.0 - 2 * i, ALU.mult, ALU.mult, [ldc, io])
                yield
        s5["cd"] = r

    ctx = ExitStack()

    def ev_h(k, ap, n, tok):
        for j in range(n):
            a = act(HT[:, k + j, :], ap[:, j, :], ACT.Copy, [tok, s5["cd"]], scale=col("norm_mix", 16 + k + j))
        return a

    steps = s5_params()
    mlp(0, A1h, A1l, ev_h, ctx, [f for _ in range(40) for f in (lambda: next(steps, None), lambda: None)])
    assert next(steps, None) is None and "cd" in s5
    ctx.close()

    ph = phase()
    ctx = ExitStack()
    CS = [sb(f"CS{i}", [128, 256], ctx=ctx) for i in range(4)]
    SN = [sb(f"SN{i}", [128, 256], ctx=ctx) for i in range(4)]
    TW = [sb(f"TW{i}", [128, 2, 256], ctx=ctx) for i in range(3)]
    WW = [sb(f"WW{i}", [128, 2, 256], ctx=ctx) for i in range(2)]
    ZZ = [sb(f"ZZ{i}", [128, 2, 256], ctx=ctx) for i in range(2)]
    XX = [sb(f"XX{i}", [128, 4, 256], ctx=ctx) for i in range(2)]
    LB = [sb(f"LB{i}", [128, 6, 128], ctx=ctx) for i in range(2)]
    HPI = NS[:, 20:21]
    hpi = P.emit("dve", None, lambda g: g.memset(HPI, math.pi / 2))
    iota = IO[:, 0:256]
    tab, rd, ht = {}, {}, {}

    def turns(m):
        k = TW[m % 3][:, 0, :]
        a = act(k, iota, ACT.Copy, [rd.get(("tw", m % 3)), io, s5["cd"]], scale=FQ[:, m:m + 1], bias=MAGIC)
        s5["k", m] = act(k, k, ACT.Copy, [a], bias=-MAGIC)

    def residue(m):
        k, v = TW[m % 3][:, 0, :], TW[m % 3][:, 1, :]
        s5["v", m] = stt(v, iota, FQ[:, m:m + 1], k, ALU.mult, ALU.subtract, [s5["k", m]])

    def tables(m):
        n, n4 = m % 3, m % 4
        k, v = TW[n][:, 0, :], TW[n][:, 1, :]
        a = act(SN[n4][:, :], v, ACT.Sin, [s5["v", m], rd.get(("cs", n4))], scale=2 * math.pi * (1 - 2e-7))
        a = act(k, v, ACT.Abs, [a])
        a = act(CS[n4][:, :], k, ACT.Sin, [a, hpi], scale=-2 * math.pi, bias=HPI)
        rd["tw", n] = a
        tab[m] = a

    def scale_rows(ct):
        h = HT[:, ct:ct + 2, :]
        ht[ct] = ht[ct + 1] = tt(h, h, RB2, ALU.mult, [nrm["rb"], nrm["k", ct], nrm["k", ct + 1]])

    def prep(ct):
        b, T, free = bank()
        for i in range(2):
            tr(T[:, 128 * i:128 * i + 128], BD[i][:, 4 * ct:4 * ct + 4, :].rearrange("p a b -> p (a b)"), [free, s5["cd"]])
        for i in range(2):
            tk = tr(T[:, 256 + 128 * i:384 + 128 * i], CD[i][:, ct, :], sig=i == 1)
        s5["t", ct] = b, T, tk

    def prep_copies(ct):
        b, T, tk = s5.pop(("t", ct))
        L_ = LB[ct % 2]
        act(L_[:, 0:4, :], T[:, :].rearrange("p (a b) -> p a b", b=128), ACT.Copy, [tk, rd.get(("lb", ct % 2))])
        r = act(L_[:, 4, :], T[:, 256:384], ACT.Copy, [tk], scale=-1.0)
        release(b, r)
        rd["lbt", ct] = act(L_[:, 5, :], IDENT, ACT.Copy, None, scale=col("b_d", ct))
        if ct % 2 == 0 and ct > 0:
            scale_rows(ct)

    def drive(m):
        ct, j = m // 4, m % 4
        b, T, free = bank()
        ps = slice(32 * j, 32 * j + 32)
        for i in range(2):
            tk = mm(T[:, 256 * i:256 * i + 256], LB[ct % 2][ps, i, :], HT[ps, ct, :], True, True,
                    [free, rd["lbt", ct], ht[ct]], i == 1)
        return b, T, tk

    def rot(v, m):
        return v[m % 4][:, :].unsqueeze(1).to_broadcast([128, 2, 256])

    def drive_turned(m, bu):
        n = m % 2
        b, T, tk = bu
        B = T[:, :].rearrange("p (a b) -> p a b", b=256)
        r1 = tt(WW[n][:, :, :], B, rot(CS, m), ALU.mult, [tk, tab[m]])
        r2 = tt(ZZ[n][:, :, :], B, rot(SN, m), ALU.mult, [tk, rd.get(("xz", n))])
        release(b, r2)
        s5["p", m] = [r1, r2]

    def drive_sum(m):
        n = m % 2
        W, Zz = WW[n], ZZ[n]
        r6 = tt(W[:, 1, :], W[:, 1, :], Zz[:, 0, :], ALU.subtract, s5["p", m])
        r5 = tt(W[:, 0, :], W[:, 0, :], Zz[:, 1, :], ALU.add, s5["p", m])
        s5["w", m] = [r5, r6]

    def scans(m):
        n = m % 2
        mg = MAG[:, m:m + 1].to_broadcast([128, 256])
        for i in range(2):
            s5["z", m] = P.emit("dve", s5["w", m], lambda g, i=i: g.tensor_tensor_scan(
                ZZ[n][:, i, :], mg, WW[n][:, i, :], 0.0, ALU.mult, ALU.add))

    def turn_back(m):
        n = m % 2
        t1 = tt(XX[n][:, 0:2, :], ZZ[n][:, :, :], rot(CS, m), ALU.mult, [s5["z", m], rd.get(("xx", n))])
        t2 = tt(XX[n][:, 2:4, :], ZZ[n][:, :, :], rot(SN, m), ALU.mult, [s5["z", m]])
        rd["cs", m % 4] = rd["xz", n] = t2
        return t2

    def readout(m, xt):
        ct, j = m // 4, m % 4
        o = G[ct % 2][32 * j:32 * j + 32, 0:256]
        cs = slice(32 * j, 32 * j + 32)
        X_ = XX[m % 2]
        for n, (l, x_) in enumerate(((2, 0), (3, 1), (4, 3), (3, 2))):
            tk = mm(o, LB[ct % 2][:, l, cs], X_[:, x_, :], n == 0, False, [rd.get(("y", ct % 2)), xt] if n == 0 else None,
                    n == 3)
        rd["xx", m % 2] = tk
        if j == 3:
            rd["lb", ct % 2] = s5["y", ct] = mm(G[ct % 2][:, 0:256], LB[ct % 2][:, 5, :], HT[:, ct, :], False, True,
                                                None, True)

    gl, gready = {}, {}

    def finish(ct):
        a = act(HT[:, ct, :], G[ct % 2][:, 0:256], ACT.Gelu_apprx_tanh, [s5["y", ct]])
        rd["y", ct % 2] = a
        s5["g", ct] = act(A1h[:, ct, :], HT[:, ct, :], ACT.Copy, [a])

    def low(ct):
        gready[ct // 2] = tt(A1l[:, ct:ct + 2, :], HT[:, ct:ct + 2, :], A1h[:, ct:ct + 2, :].bitcast(F32), ALU.subtract,
                             s5["g", ct + 1])

    def glu_rows(ct, i):
        if ct % 4 == 0 and i == 0:
            gl["w"] = raw_chunk("gl0")
        c, w, ar = gl["w"]
        tk = gl["tok", i] = mm(G[2 + i][:, :], HT[:, ct, 128 * i:128 * i + 128], w[:, ct % 4, :], ct == 0, ct == 15,
                               [ar, s5["g", ct]], i == 1 or ct == 15)
        if i == 1:
            if ct % 4 == 3:
                free_raw(c, tk)
            if ct in (7, 11, 13, 15):
                split_next()

    prep(0)
    prep_copies(0)
    turns(0)
    turns(1)
    while soon:
        soon.popleft()()
    scale_rows(0)
    residue(0)
    residue(1)
    tables(0)
    turns(2)
    residue(2)
    tables(1)
    tables(2)
    turns(3)
    bus = {0: drive(0), 1: drive(1)}
    drive_turned(0, bus.pop(0))
    drive_sum(0)
    early, later = {}, {}
    for m in range(64):
        ct, j = m // 4, m % 4
        if m + 3 < 64:
            residue(m + 3)
        if m + 1 < 64:
            drive_turned(m + 1, bus.pop(m + 1))
        if m + 2 < 64:
            if j == 0 and ct < 15:
                prep(ct + 1)
            bus[m + 2] = drive(m + 2)
        for fn in early.pop(m, []):
            fn()
        scans(m)
        if m + 1 < 64:
            drive_sum(m + 1)
        xt = turn_back(m)
        if m + 3 < 64:
            tables(m + 3)
        if m + 4 < 64:
            turns(m + 4)
        if j == 1 and ct < 15:
            prep_copies(ct + 1)
        readout(m, xt)
        for fn in later.pop(m, []):
            fn()
        if j == 3:
            later.setdefault(m + 3, []).append(lambda ct=ct: finish(ct))
            early[m + 6] = [lambda ct=ct: glu_rows(ct, 0)]
            early[m + 7] = [lambda ct=ct: glu_rows(ct, 1)]
            if ct % 2:
                later.setdefault(m + 7, []).append(lambda ct=ct: low(ct - 1))
    for m in range(64, 64 + 8):
        for fn in later.pop(m, []) + early.pop(m, []):
            fn()
    pair_next[0] = 0
    pair_free[0] = [rd["y", 0], rd["y", 1]]
    ctx.close()
    ctxs.close()

    ctx = ExitStack()
    A3h = sb("A3h", [128, 16, 256], F32R, ctx)
    A3l = sb("A3l", [128, 16, 256], F32R, ctx)
    VL = [sb(f"VL{i}", [128, 512], ctx=ctx) for i in range(2)]
    SGt = [sb(f"SGt{i}", [128, 512], ctx=ctx) for i in range(2)]
    GR = sb("GR2", [128, D], ctx=ctx)
    ph = phase()
    ld = P.dma("act", ph, GR[:, :], t["final2_row"], "m_row")
    ev_m1 = to_A(A3h, A3l, lambda k: col("norm_mlp", 16 + k))
    vt = [None, None]
    vr = [None, None]

    def ev_l(ap, i, tok):
        vt[i] = act(VL[i][:, :], ap, ACT.Copy, [tok, vr[i]])
        return vt[i]

    def ev_g(n0):
        def ev(ap, i, tok):
            a = act(SGt[i][:, :], ap, ACT.Sigmoid, [tok, vr[i]])
            d = tt(VL[i][:, :], VL[i][:, :], SGt[i][:, :], ALU.mult, [a, vt[i]])
            xs = X[:, i, n0:n0 + 512]
            r = tt(xs, xs, VL[i][:, :], ALU.add, [d, x_tok[i].get(n0)])
            x_tok[i][n0] = r
            vr[i] = r
            if i == 1:
                bg.extend(norm_steps(n0 // 512, ev_m1))
            return a
        return ev

    pair_free[1] = [ev_l(G[2 + i][:, :], i, gl["tok", i]) for i in range(2)]
    for i in range(4):
        if i:
            gemm(f"gl{i}", A1h, A1l, 16, False, ev_l, None, 1)
        gemm(f"gg{i}", A1h, A1l, 16, False, ev_g(512 * i), None, 1, kready=None if i else lambda kt: gready[kt // 2])
    flush_bg()
    norm_finish(rows=False)
    gained = {}

    def gain(k):
        def run():
            for i in range(2):
                xs = X[:, i, 512 * k:512 * k + 512]
                gained[i, k] = tt(xs, xs, GR[:, 512 * k:512 * k + 512], ALU.mult, [nrm["sq", i, k], ld])
        return run

    mlp(1, A3h, A3l, None, ctx, then=[[gain(k)] for k in range(3)] + [()])
    assert state["chunk"] == len(chunks) and state["split"] == len(halves)

    outs = []
    ov = t["out"][0].rearrange("(i p) n -> p i n", p=128)
    for k in (3, 0, 1, 2):
        r = []
        for i in range(2):
            xs = X[:, i, 512 * k:512 * k + 512]
            if k == 3:
                r.append(stt(xs, xs, RC[i], GR[:, 512 * k:512 * k + 512], ALU.mult, ALU.mult, [nrm["r"], ld]))
            elif i == 0 or k == 0:
                r.append(act(xs, xs, ACT.Copy, [nrm["r"], gained[i, k]], scale=RC[i]))
            else:
                r.append(ts(xs, xs, RC[i], None, ALU.mult, waits=[nrm["r"], gained[i, k]]))
        outs.append(P.dma("sp", r, ov[:, :, 512 * k:512 * k + 512], X[:, :, 512 * k:512 * k + 512], f"out{k}"))
    P.wait("sp", outs)
    ctx.close()

    used = set()
    for e in P.ENG:
        for item in P.q[e]:
            used.add(item[1] if item[0] == "wait" else item[2])
    used.discard(None)
    sems = {s: top.enter_context(nc.semaphore(f"s_{s}")) for s in sorted(used)}
    block = top.enter_context(nc.Block())

    @block.sync
    def _(eng):
        P.play("sp", eng, sems)

    @block.gpsimd
    def _(eng):
        P.play("pool", eng, sems)

    @block.scalar
    def _(eng):
        P.play("act", eng, sems)

    @block.vector
    def _(eng):
        P.play("dve", eng, sems)

    @block.tensor
    def _(eng):
        P.play("pe", eng, sems)

    top.close()


def _constants():
    import numpy as _np

    c = _np.zeros((128, NCONST), _np.float32)
    p = _np.arange(128)[:, None]
    s = _np.arange(256)[None, :]
    c[:, 0:128] = _np.eye(128)
    c[:, 128:256] = 1.0
    for base, f in ((256, lambda q, k: k <= q), (640, lambda q, k: k // 64 <= q // 64)):
        c[:, base:base + 128] = _np.where(f(p, s[:, 0:128]), 0.0, NEG)
        c[:, base + 128:base + 384] = _np.where(f(p + 128, s), 0.0, NEG)
    c[:, 1024:1280] = s
    c[:, 1280:1281] = (p // 16) % 2 == 0
    c[:, 1281:1282] = (p // 16) % 2 == 1
    return c


def kernel(**inputs):
    import numpy as _np
    import concourse.bacc as _bacc
    from concourse import mybir as _mybir
    from concourse.bass_utils import run_bass_kernel_spmd as _run

    a = {k: _np.asarray(v) for k, v in inputs.items()}

    def vec(v):
        v = v.reshape(-1)
        return v.reshape(-1, 128).T

    cols = _np.concatenate([
        vec(a["even_norm"]), vec(a["even_b_glu"]),
        a["even_w_dw"][0].T.reshape(8, 128, 31).transpose(1, 0, 2).reshape(128, 248),
        vec(a["even_b_dw"]), vec(a["even_conv_ln_g"]), vec(a["even_conv_ln_b"]), vec(a["even_b_pw"]),
        vec(a["odd_norm"]), vec(a["odd_q_norm"]),
        _np.tile(a["odd_ik_ln_g"].reshape(-1), 2).reshape(128, 1), _np.tile(a["odd_ik_ln_b"].reshape(-1), 2).reshape(128, 1),
        vec(a["norm_mix_2"]), vec(a["norm_mlp_2"]), vec(a["a_subln_2"]), vec(a["a_lambda_2"]), vec(a["b_d_2"]),
        vec(a["b_a_re_2"]), vec(a["b_a_im_2"]),
        _np.repeat(a["b_log_dt_2"].reshape(-1), 64).reshape(64, 128).T, vec(a["final_norm"]),
    ], axis=1)
    arrays = {
        "cols": _np.ascontiguousarray(cols),
        "consts": _constants(),
        "kv_row": _np.ascontiguousarray(_np.broadcast_to(a["odd_kv_norm"].reshape(1, 256), (128, 256))),
        "final_row": _np.ascontiguousarray(_np.broadcast_to(a["final_norm"].reshape(1, 2048), (128, 2048))),
        "final2_row": _np.ascontiguousarray(_np.broadcast_to(a["norm_final_2"].reshape(1, 2048), (128, 2048))),
        "s5_b": _np.ascontiguousarray(_np.stack([a[n].reshape(64, 128, 16).transpose(1, 0, 2) for n in ("b_b_re_2", "b_b_im_2")])),
        "s5_c": _np.ascontiguousarray(_np.stack([a[n].reshape(16, 128, 64).transpose(1, 0, 2) for n in ("b_c_re_2", "b_c_im_2")])),
    }
    for n in ("x", "even_w_in", "even_w_pw", "even_w_out", "odd_w_in", "odd_w_qb", "odd_w_uk", "odd_w_uv", "odd_w_iq",
              "odd_w_out", "a_w_in_2", "a_w_out_2", "b_w_glu_2", "mlp_w1_2", "mlp_w2_2"):
        arrays[n] = _np.ascontiguousarray(a[n])
    nc = _bacc.Bacc("TRN2", target_bir_lowering=False, num_devices=1)
    t = {n: nc.dram_tensor(f"in_{n}", v.shape, _mybir.dt.from_np(v.dtype), kind="ExternalInput").ap()
         for n, v in arrays.items()}
    t["out"] = nc.dram_tensor("out_0", (1, 256, 2048), _mybir.dt.from_np(_np.dtype("float32")), kind="ExternalOutput").ap()
    build_program(nc, t)
    r = _run(nc, [{f"in_{n}": v for n, v in arrays.items()}], core_ids=[0])
    return r.results[0]["out_0"]
```
